# Optimizing a Trainium2 kernel written in Bass

```python
import jax, jax.numpy as jnp
from jax import lax
import numpy as np
import math

D_MODEL = 2048
BATCH = 1
SEQ = 256
DEPTH = 1

N_BRANCH = 4
BRANCH_WIDTH = D_MODEL // 4
LRU_WIDTH = BRANCH_WIDTH
LRU_BLOCKS = 8
LRU_BLOCK_DIM = LRU_WIDTH // LRU_BLOCKS
LRU_CONV = 4
LRU_C = 8.0
POOL_WIDTH = BRANCH_WIDTH
POOL_WINDOWS = (2, 4, 8, 16)
POOL_GROUPS = 4
POOL_GROUP_DIM = POOL_WIDTH // POOL_GROUPS
SCONV_WIDTH = BRANCH_WIDTH
SCONV_K = 3
ATTN_HEADS = 8
HEAD_DIM = BRANCH_WIDTH // ATTN_HEADS
ATTN_WIDTH = ATTN_HEADS * HEAD_DIM
Q_BLOCK = 128
D_FF = 4 * D_MODEL
EPS = 1e-6
IN_SIZES = (LRU_WIDTH, POOL_WIDTH, 3 * SCONV_WIDTH, 3 * ATTN_WIDTH, ATTN_HEADS, N_BRANCH * D_MODEL)
N_IN = sum(IN_SIZES)


def _split_points():
    return [int(v) for v in np.cumsum(IN_SIZES)[:-1]]

def rms_norm(x, g):
    xf = x.astype(jnp.float32)
    y = xf * lax.rsqrt(jnp.mean(xf * xf, axis=-1, keepdims=True) + EPS)
    return (y * g.astype(jnp.float32)).astype(x.dtype)

def causal_depthwise_conv(x, w):
    k_width = w.shape[0]
    s = x.shape[1]
    xp = jnp.pad(x, ((0, 0), (k_width - 1, 0), (0, 0)))
    return sum(w[k] * xp[:, k:k + s] for k in range(k_width))

def rglru_branch(xa, conv_w, conv_b, wr, br, wi, bi, lam):
    b, s, _ = xa.shape
    u = causal_depthwise_conv(xa, conv_w) + conv_b
    ub = u.reshape(b, s, LRU_BLOCKS, LRU_BLOCK_DIM)
    r = jax.nn.sigmoid(jnp.einsum('bshi,hij->bshj', ub, wr).reshape(b, s, LRU_WIDTH) + br)
    gi = jax.nn.sigmoid(jnp.einsum('bshi,hij->bshj', ub, wi).reshape(b, s, LRU_WIDTH) + bi)
    log_a = (-LRU_C * r.astype(jnp.float32)) * jax.nn.softplus(-lam.astype(jnp.float32))
    a = jnp.exp(log_a)
    inp = jnp.sqrt(-jnp.expm1(2.0 * log_a)) * (gi * u).astype(jnp.float32)

    def combine(c1, c2):
        a1, b1 = c1
        a2, b2 = c2
        return a1 * a2, a2 * b1 + b2

    _, h = lax.associative_scan(combine, (a, inp), axis=1)
    return h.astype(xa.dtype)

def pool_branch(xp, w_grp, scale):
    b, s, _ = xp.shape
    xf = xp.astype(jnp.float32)
    csum = jnp.pad(jnp.cumsum(xf, axis=1), ((0, 0), (1, 0), (0, 0)))
    t = jnp.arange(s)
    outs = []
    for gidx, win in enumerate(POOL_WINDOWS):
        sl = slice(gidx * POOL_GROUP_DIM, (gidx + 1) * POOL_GROUP_DIM)
        start = jnp.maximum(t + 1 - win, 0)
        win_sum = csum[:, 1:, sl] - csum[:, start, sl]
        count = jnp.minimum(t + 1, win).astype(jnp.float32)[None, :, None]
        outs.append(win_sum / count - xf[:, :, sl])
    pooled = jnp.stack(outs, axis=2)
    mixed = jnp.einsum('bsgi,gij->bsgj', pooled, w_grp.astype(jnp.float32)).reshape(b, s, POOL_WIDTH)
    return (mixed * scale.astype(jnp.float32)).astype(xp.dtype)

def shortconv_branch(xsc, w):
    gate_b, gate_c, xc = jnp.split(xsc, 3, axis=-1)
    return gate_b * causal_depthwise_conv(gate_c * xc, w)

def forgetting_attention(qkv, f_logit, f_bias, q_g, k_g):
    b, s, _ = qkv.shape
    q, k, v = jnp.split(qkv, 3, axis=-1)
    q = rms_norm(q.reshape(b, s, ATTN_HEADS, HEAD_DIM), q_g)
    k = rms_norm(k.reshape(b, s, ATTN_HEADS, HEAD_DIM), k_g)
    v = v.reshape(b, s, ATTN_HEADS, HEAD_DIM)
    log_f = jax.nn.log_sigmoid((f_logit + f_bias).astype(jnp.float32))
    cum = jnp.cumsum(log_f, axis=1).transpose(0, 2, 1)
    n_blk = s // Q_BLOCK
    qb = q.reshape(b, n_blk, Q_BLOCK, ATTN_HEADS, HEAD_DIM).transpose(1, 0, 2, 3, 4)
    cqb = cum.reshape(b, ATTN_HEADS, n_blk, Q_BLOCK).transpose(2, 0, 1, 3)
    key_pos = jnp.arange(s)
    scale = HEAD_DIM ** -0.5

    def one_block(args):
        qi, cqi, blk = args
        logits = jnp.einsum('bqhd,bkhd->bhqk', qi, k).astype(jnp.float32) * scale
        logits = logits + (cqi[..., :, None] - cum[..., None, :])
        q_pos = blk * Q_BLOCK + jnp.arange(Q_BLOCK)
        logits = jnp.where(key_pos[None, :] <= q_pos[:, None], logits, -jnp.inf)
        p = jax.nn.softmax(logits, axis=-1)
        return jnp.einsum('bhqk,bkhd->bqhd', p.astype(v.dtype), v)

    out = lax.map(one_block, (qb, cqb, jnp.arange(n_blk)))
    return out.transpose(1, 0, 2, 3, 4).reshape(b, s, ATTN_WIDTH)

def first_inputs(seed: int = 0) -> dict:
    key = jax.random.key(seed)
    ks = jax.random.split(key, 24)
    L, D, W = DEPTH, D_MODEL, BRANCH_WIDTH
    nrm = lambda k, shape, fan: jax.random.normal(k, shape, jnp.float32) * (fan ** -0.5)
    u = jax.random.uniform(ks[9], (L, LRU_WIDTH), jnp.float32, 0.9, 0.999)
    a0 = u ** (1.0 / LRU_C)
    return {
        "x": jax.random.normal(ks[0], (BATCH, SEQ, D), jnp.float32),
        "norm_mix_g": 1.0 + 0.1 * jax.random.normal(ks[1], (L, D), jnp.float32),
        "w_in": nrm(ks[2], (L, D, N_IN), D),
        "lru_conv_w": nrm(ks[3], (L, LRU_CONV, LRU_WIDTH), LRU_CONV),
        "lru_conv_b": 0.02 * jax.random.normal(ks[4], (L, LRU_WIDTH), jnp.float32),
        "lru_wr": nrm(ks[5], (L, LRU_BLOCKS, LRU_BLOCK_DIM, LRU_BLOCK_DIM), LRU_BLOCK_DIM),
        "lru_br": 0.02 * jax.random.normal(ks[6], (L, LRU_WIDTH), jnp.float32),
        "lru_wi": nrm(ks[7], (L, LRU_BLOCKS, LRU_BLOCK_DIM, LRU_BLOCK_DIM), LRU_BLOCK_DIM),
        "lru_bi": 0.02 * jax.random.normal(ks[8], (L, LRU_WIDTH), jnp.float32),
        "lru_lambda": jnp.log(a0) - jnp.log1p(-a0),
        "pool_w": nrm(ks[10], (L, POOL_GROUPS, POOL_GROUP_DIM, POOL_GROUP_DIM), POOL_GROUP_DIM),
        "pool_scale": 1.0 + 0.1 * jax.random.normal(ks[11], (L, POOL_WIDTH), jnp.float32),
        "sconv_w": nrm(ks[12], (L, SCONV_K, SCONV_WIDTH), SCONV_K),
        "q_norm_g": 1.0 + 0.1 * jax.random.normal(ks[13], (L, HEAD_DIM), jnp.float32),
        "k_norm_g": 1.0 + 0.1 * jax.random.normal(ks[14], (L, HEAD_DIM), jnp.float32),
        "forget_b": jax.random.uniform(ks[15], (L, ATTN_HEADS), jnp.float32, 1.0, 5.0),
        "w_branch": nrm(ks[16], (L, N_BRANCH, W, D), W),
        "w_out": nrm(ks[17], (L, D, D), D),
        "norm_mlp_g": 1.0 + 0.1 * jax.random.normal(ks[18], (L, D), jnp.float32),
        "w_mlp_up": nrm(ks[19], (L, D, D_FF), D),
        "w_mlp_down": nrm(ks[20], (L, D_FF, D), D_FF),
    }

def first_block(x, norm_mix_g, w_in, lru_conv_w, lru_conv_b, lru_wr, lru_br, lru_wi, lru_bi,
              lru_lambda, pool_w, pool_scale, sconv_w, q_norm_g, k_norm_g, forget_b,
              w_branch, w_out, norm_mlp_g, w_mlp_up, w_mlp_down):
    b, s, d = x.shape
    split_pts = _split_points()
    for l in range(DEPTH):
        xn = rms_norm(x, norm_mix_g[l])
        proj = xn @ w_in[l]
        xa, xpool, xsc, qkv, f_logit, gate_logits = jnp.split(proj, split_pts, axis=-1)
        y_a = rglru_branch(xa, lru_conv_w[l], lru_conv_b[l], lru_wr[l], lru_br[l],
                           lru_wi[l], lru_bi[l], lru_lambda[l])
        y_b = pool_branch(xpool, pool_w[l], pool_scale[l])
        y_c = shortconv_branch(xsc, sconv_w[l])
        y_d = forgetting_attention(qkv, f_logit, forget_b[l], q_norm_g[l], k_norm_g[l])
        ys = jnp.stack([y_a, y_b, y_c, y_d], axis=2)
        branches = jnp.einsum('bskw,kwd->bskd', ys, w_branch[l])
        gates = jax.nn.sigmoid(gate_logits.reshape(b, s, N_BRANCH, d))
        merged = jnp.sum(gates * branches, axis=2)
        x = x + merged @ w_out[l]
        h = rms_norm(x, norm_mlp_g[l]) @ w_mlp_up[l]
        x = x + jnp.square(jax.nn.relu(h)) @ w_mlp_down[l]
    return x


HEAD_DIM_2 = 128
DIL_GROUPS = ((128, 1), (512, 4), (2048, 16))
HEADS_PER_DIL_GROUP = 4
N_HEADS_A = HEADS_PER_DIL_GROUP * len(DIL_GROUPS)
N_HEADS_B = 4
WIDTH_A = N_HEADS_A * HEAD_DIM_2
WIDTH_B = N_HEADS_B * HEAD_DIM_2
A_OUT = HEADS_PER_DIL_GROUP * HEAD_DIM_2
D_IN = 3 * WIDTH_A + 3 * WIDTH_B + 2 * D_MODEL
D_FF_2 = 5632
CONV_WIDTH = 3
PLE_DIM = 256
BLOCK = 128
RMS_EPS = 1e-6
ALIBI_MAX = 8.0


def rmsnorm(x, g):
    xf = x.astype(jnp.float32)
    y = xf * lax.rsqrt(jnp.mean(xf * xf, axis=-1, keepdims=True) + RMS_EPS)
    return (y * g.astype(jnp.float32)).astype(x.dtype)

def alibi_slopes(n):
    return jnp.exp2(-ALIBI_MAX * jnp.arange(1, n + 1, dtype=jnp.float32) / n)

def dilated_window_group(q, k, v, window, dilation, slopes):
    b, s, hg, dh = q.shape
    n_back = window // dilation
    span = dilation * BLOCK
    s_pad = -(-s // span) * span
    L = s_pad // dilation
    nb = L // BLOCK

    def to_blocks(t):
        t = jnp.pad(t, ((0, 0), (0, s_pad - s), (0, 0), (0, 0)))
        t = t.reshape(b, L, dilation, hg, dh).transpose(0, 2, 3, 1, 4)
        return t.reshape(b, dilation, hg, nb, BLOCK, dh)

    def with_prev(t):
        prev = jnp.pad(t, ((0, 0), (0, 0), (0, 0), (1, 0), (0, 0), (0, 0)))[:, :, :, :-1]
        return jnp.concatenate([prev, t], axis=4)

    qb = to_blocks(q)
    kk = with_prev(to_blocks(k))
    vv = with_prev(to_blocks(v))
    scores = jnp.einsum('brhnqe,brhnke->brhnqk', qb, kk).astype(jnp.float32) * (1.0 / math.sqrt(dh))
    qi = jnp.arange(BLOCK)[:, None]
    ki = jnp.arange(2 * BLOCK)[None, :]
    steps = BLOCK + qi - ki
    valid = (steps >= 0) & (steps <= n_back)
    first = (jnp.arange(nb) == 0)[:, None, None]
    valid = valid[None] & ~(first & (ki < BLOCK)[None])
    bias = -slopes[:, None, None] * (steps * dilation).astype(jnp.float32)[None]
    scores = scores + bias[None, None, :, None]
    scores = jnp.where(valid[None, None, None], scores, -jnp.inf)
    lse = jax.nn.logsumexp(scores, axis=-1)
    probs = jnp.exp(scores - lse[..., None])
    out = jnp.einsum('brhnqk,brhnke->brhnqe', probs.astype(v.dtype), vv)

    def from_blocks(t):
        t = t.reshape(b, dilation, hg, L, *t.shape[5:])
        t = jnp.moveaxis(t, 3, 1)
        return t.reshape(b, s_pad, hg, *t.shape[4:])[:, :s]

    return from_blocks(out), from_blocks(lse)

def dilated_mixture_attention(q, k, v):
    b, s = q.shape[:2]
    slopes = alibi_slopes(N_HEADS_A)
    outs, lses = [], []
    for g, (window, dilation) in enumerate(DIL_GROUPS):
        sl = slice(g * HEADS_PER_DIL_GROUP, (g + 1) * HEADS_PER_DIL_GROUP)
        o, l = dilated_window_group(q[:, :, sl], k[:, :, sl], v[:, :, sl], window, dilation, slopes[sl])
        outs.append(o)
        lses.append(l)
    alpha = jax.nn.softmax(jnp.stack(lses), axis=0)
    y = jnp.sum(alpha[..., None] * jnp.stack(outs).astype(jnp.float32), axis=0)
    return y.reshape(b, s, A_OUT).astype(q.dtype)

def stick_breaking_attention(q, k, v):
    b, s, h, dh = q.shape
    nb = s // BLOCK
    qt = q.transpose(0, 2, 1, 3)
    kt = k.transpose(0, 2, 1, 3)
    vt = v.transpose(0, 2, 1, 3)
    scale = 1.0 / math.sqrt(dh)
    idx = jnp.arange(BLOCK)
    tri_within = (idx[:, None] > idx[None, :]).astype(jnp.float32)
    diag_before = idx[None, :] < idx[:, None]
    outs = []
    for n in range(nb):
        c = n + 1
        kl = c * BLOCK
        qblk = qt[:, :, n * BLOCK:(n + 1) * BLOCK]
        z = jnp.einsum('bhqe,bhke->bhqk', qblk, kt[:, :, :kl]).astype(jnp.float32) * scale
        before = jnp.concatenate([jnp.ones((BLOCK, n * BLOCK), dtype=bool), diag_before], axis=1)
        ln = jnp.where(before, jax.nn.log_sigmoid(-z), 0.0)
        lnc = ln.reshape(b, h, BLOCK, c, BLOCK)
        within = jnp.einsum('bhqcj,ji->bhqci', lnc, tri_within)
        tot = jnp.sum(lnc, axis=-1)
        cidx = jnp.arange(c)
        after = jnp.einsum('bhqc,cd->bhqd', tot, (cidx[:, None] > cidx[None, :]).astype(jnp.float32))
        logw = z.reshape(b, h, BLOCK, c, BLOCK) + lnc + within + after[..., None]
        w = jnp.where(before, jnp.exp(logw.reshape(b, h, BLOCK, kl)), 0.0)
        outs.append(jnp.einsum('bhqk,bhke->bhqe', w.astype(v.dtype), vt[:, :, :kl]))
    out = jnp.concatenate(outs, axis=2)
    return out.transpose(0, 2, 1, 3).reshape(b, s, h * dh)

def causal_depthwise_conv_2(x, w, bias):
    s = x.shape[1]
    xp = jnp.pad(x, ((0, 0), (CONV_WIDTH - 1, 0), (0, 0)))
    y = bias + w[0] * xp[:, 0:s]
    for j in range(1, CONV_WIDTH):
        y = y + w[j] * xp[:, j:j + s]
    return y

def second_inputs(seed: int = 0) -> dict:
    key = jax.random.key(seed)
    ks = jax.random.split(key, 20)
    f32 = jnp.float32

    def nrm(k, shape, scale):
        return jax.random.normal(k, shape, f32) * scale

    def gain(k):
        return 1.0 + 0.05 * jax.random.normal(k, (DEPTH, D_MODEL), f32)

    return {
        'x': nrm(ks[0], (BATCH, SEQ, D_MODEL), 1.0),
        'p': nrm(ks[1], (DEPTH, BATCH, SEQ, PLE_DIM), 1.0),
        'g_mix_pre': gain(ks[2]),
        'w_in': nrm(ks[3], (DEPTH, D_MODEL, D_IN), D_MODEL ** -0.5),
        'w_branch_a': nrm(ks[4], (DEPTH, A_OUT, D_MODEL), A_OUT ** -0.5),
        'w_branch_b': nrm(ks[5], (DEPTH, WIDTH_B, D_MODEL), WIDTH_B ** -0.5),
        'w_out': nrm(ks[6], (DEPTH, D_MODEL, D_MODEL), D_MODEL ** -0.5),
        'g_mix_post': gain(ks[7]),
        'g_ffn_pre': gain(ks[8]),
        'w_up': nrm(ks[9], (DEPTH, D_MODEL, 2 * D_FF_2), D_MODEL ** -0.5),
        'conv_w': nrm(ks[10], (DEPTH, CONV_WIDTH, 2 * D_FF_2), CONV_WIDTH ** -0.5),
        'conv_b': nrm(ks[11], (DEPTH, 2 * D_FF_2), 0.01),
        'w_down': nrm(ks[12], (DEPTH, D_FF_2, D_MODEL), D_FF_2 ** -0.5),
        'g_ffn_post': gain(ks[13]),
        'w_ple_in': nrm(ks[14], (DEPTH, PLE_DIM, D_MODEL), PLE_DIM ** -0.5),
        'w_ple_gate': nrm(ks[15], (DEPTH, D_MODEL, D_MODEL), D_MODEL ** -0.5),
    }

def second_block(x, p, g_mix_pre, w_in, w_branch_a, w_branch_b, w_out, g_mix_post, g_ffn_pre, w_up, conv_w, conv_b, w_down, g_ffn_post, w_ple_in, w_ple_gate):
    b, s, _ = x.shape
    splits = [WIDTH_A, 2 * WIDTH_A, 3 * WIDTH_A,
              3 * WIDTH_A + WIDTH_B, 3 * WIDTH_A + 2 * WIDTH_B, 3 * WIDTH_A + 3 * WIDTH_B,
              3 * WIDTH_A + 3 * WIDTH_B + D_MODEL]
    h = x
    for i in range(DEPTH):
        u = rmsnorm(h, g_mix_pre[i])
        proj = u @ w_in[i]
        qa, ka, va, qb, kb, vb, gla, glb = jnp.split(proj, splits, axis=-1)
        heads_a = lambda t: t.reshape(b, s, N_HEADS_A, HEAD_DIM_2)
        heads_b = lambda t: t.reshape(b, s, N_HEADS_B, HEAD_DIM_2)
        ya = dilated_mixture_attention(heads_a(qa), heads_a(ka), heads_a(va)) @ w_branch_a[i]
        yb = stick_breaking_attention(heads_b(qb), heads_b(kb), heads_b(vb)) @ w_branch_b[i]
        gate_a = jax.nn.sigmoid(gla.astype(jnp.float32)).astype(h.dtype)
        gate_b = jax.nn.sigmoid(glb.astype(jnp.float32)).astype(h.dtype)
        mix = (gate_a * ya + gate_b * yb) @ w_out[i]
        h = h + rmsnorm(mix, g_mix_post[i])
        u = rmsnorm(h, g_ffn_pre[i])
        up = causal_depthwise_conv_2(u @ w_up[i], conv_w[i], conv_b[i])
        gate_ff, value = jnp.split(up, [D_FF_2], axis=-1)
        f = (jax.nn.gelu(gate_ff, approximate=True) * value) @ w_down[i]
        h = h + rmsnorm(f, g_ffn_post[i])
        e = p[i] @ w_ple_in[i]
        h = h + jax.nn.sigmoid((h @ w_ple_gate[i]).astype(jnp.float32)).astype(h.dtype) * e
    return h


def setup_inputs(seed=0):
    out = dict(first_inputs(seed))
    for name, value in second_inputs(seed + 1).items():
        if name != "x":
            out[name + "_2"] = value
    return out


def reference(
    x, norm_mix_g, w_in, lru_conv_w, lru_conv_b, lru_wr, lru_br, lru_wi, lru_bi, lru_lambda,
    pool_w, pool_scale, sconv_w, q_norm_g, k_norm_g, forget_b, w_branch, w_out, norm_mlp_g,
    w_mlp_up, w_mlp_down, p_2, g_mix_pre_2, w_in_2, w_branch_a_2, w_branch_b_2, w_out_2,
    g_mix_post_2, g_ffn_pre_2, w_up_2, conv_w_2, conv_b_2, w_down_2, g_ffn_post_2, w_ple_in_2,
    w_ple_gate_2,
):
    x = first_block(
        x, norm_mix_g, w_in, lru_conv_w, lru_conv_b, lru_wr, lru_br, lru_wi, lru_bi, lru_lambda,
        pool_w, pool_scale, sconv_w, q_norm_g, k_norm_g, forget_b, w_branch, w_out, norm_mlp_g,
        w_mlp_up, w_mlp_down,
    )
    return second_block(
        x, p_2, g_mix_pre_2, w_in_2, w_branch_a_2, w_branch_b_2, w_out_2, g_mix_post_2,
        g_ffn_pre_2, w_up_2, conv_w_2, conv_b_2, w_down_2, g_ffn_post_2, w_ple_in_2,
        w_ple_gate_2,
    )


_drawn_inputs = setup_inputs


def setup_inputs(seed=0):
    import zlib

    import numpy as np

    out = dict(_drawn_inputs(seed))
    spreads = {}
    factors = {'lru_br': 40.266, 'lru_bi': 28.859, 'q_norm_g': 4.137, 'k_norm_g': 4.253, 'conv_b_2': 8.0}
    for name, (base, spread) in spreads.items():
        noise = np.random.default_rng([zlib.crc32(name.encode()), seed]).standard_normal(out[name].shape)
        drawn = base * np.exp(spread * noise) if base else spread * noise
        out[name] = __import__('jax').numpy.asarray(drawn.astype(out[name].dtype))
    for name, factor in factors.items():
        out[name] = (out[name] * factor).astype(out[name].dtype)
    return out
```

```python
from contextlib import ExitStack

import numpy as np
import concourse.bass as bass
from concourse import mybir

F32 = mybir.dt.float32
F32R = mybir.dt.float32r
ACT = mybir.ActivationFunctionType
ALU = mybir.AluOpType
AX = mybir.AxisListType

P = 128
S = 256
D = 2048
KT = D // P
BW = 512
BT = BW // P
DFF = 8192
DFF2 = 5632
N_F = 4096
N_G = 4104
HEADS = 8
HD = 64
N_G2 = 6144
SLOTS = 4
GROUPS = 3
EPS = 1e-6
NEG = -1.0e30
RING = 4
TINY = 2.0 ** -116
HD2_SCALE = 128.0 ** -0.5


def param_columns():
    sizes = [("g_mix", 16), ("g_mlp", 16), ("g_mix_pre2", 16), ("g_mix_post2", 16), ("g_ffn_pre2", 16),
             ("g_ffn_post2", 16), ("lru_conv_w", 16), ("lru_conv_b", 4), ("lru_br", 4), ("lru_bi", 4),
             ("lru_lambda", 4), ("pool_scale", 4), ("sconv_w", 12), ("q_g", 1), ("k_g", 1), ("forget_b", 1),
             ("conv_w2", 3 * 88), ("conv_b2", 88)]
    at, cols = 0, {}
    for name, n in sizes:
        cols[name] = at
        at += n
    return cols, at


def slope(head):
    return float(np.float32(2.0) ** np.float32(-8.0 * (head + 1) / (SLOTS * GROUPS)))


def constants():
    p = np.arange(P)[:, None]
    f = np.arange(P)[None, :]
    ident = (p == f)
    ones = np.ones((P, P))
    common = np.concatenate([ident, ones], 1).astype(np.float32)
    same_head = (p // HD == f // HD)
    causal = np.where(f <= p, 0.0, NEG)
    mask3 = np.concatenate([causal, np.zeros((P, P)), causal], 1)
    inv = np.broadcast_to(1.0 / (np.arange(16) + 1.0), (P, 16))
    first = np.concatenate([same_head, mask3, inv], 1).astype(np.float32)
    sel = np.zeros((HEADS, HEADS, P), np.float32)
    for h in range(HEADS):
        sel[h, h] = 1.0
    dist = (P + p) - np.arange(2 * P)[None, :]
    groups = []
    for span, dil in ((128, 1), (512, 4), (2048, 16)):
        ok = (dist >= 0) & (dist % dil == 0) & (dist <= span)
        groups.append(np.where(ok, -dist, NEG))
    strict = p < f
    before01 = np.concatenate([strict, np.ones((P, P))], 1)
    before_neg = np.where(before01 > 0, 0.0, NEG)
    later = (p > f)
    second = np.concatenate(groups + [before01, before_neg, later], 1).astype(np.float32)
    return common, first, sel.reshape(HEADS, HEADS * P), second


class Phase:

    def __init__(self, kind, units, U, ppu, name, quarter=0, group=0, half=0):
        self.kind, self.units, self.U, self.ppu, self.name = kind, units, U, ppu, name
        self.quarter, self.group, self.half = quarter, group, half
        self.piece0 = self.unit0 = self.bodies = 0
        self.count0 = {}


ADDS = {
    "scaled": {"gate": [1, 1], "branch4": [0, 1, 1, 1], "branch4s": [0, 1, 1, 1], "branch2": [0, 1, 0, 1],
               "branch2s": [0, 1, 0, 1], "up": [1, 1], "upconv": [1, 1], "final": [1, 1]},
    "acted": {"up": [1, 1], "upconv": [1, 1], "final": [1, 1]},
    "conv_base": {"upconv": [1, 1]},
    "conv_tap": {"upconv": [2, 2]},
    "conv_done": {"upconv": [0, 1]},
    "merged": {"branch4s": [0, 0, 0, 1], "branch2s": [0, 1, 0, 1], "resid": [1, 1], "accsq": [1, 1, 1, 1]},
    "high_out": {"branch4s": [0, 0, 0, 1], "branch2s": [0, 1, 0, 1], "up": [1, 1], "resid": [1, 1],
                 "upconv": [0, 1]},
    "squared": {"resid": [1, 1], "mix": [1, 1], "accsq": [1, 1, 1, 1]},
    "sq_added": {"resid": [1, 1], "mix": [1, 1], "accsq": [1, 1, 1, 1]},
}


def plan():
    ph = [Phase("proj", 16, 2, 4, name="proj")]
    for q in range(4):
        ph.append(Phase("gate", 8, 2, 4, name=f"gates_a{q}", quarter=q))
        ph.append(Phase("branch4s" if q == 3 else "branch4", 8, 4, 1, name=f"mix_a{q}", quarter=q))
    ph.append(Phase("resid", 8, 2, 4, name="w_out"))
    for g in range(4):
        ph.append(Phase("up", 8, 2, 4, name=f"mlp_up{g}", group=g))
        ph.append(Phase("resid" if g == 3 else "accum", 8, 2, 4, name=f"mlp_down{g}", group=g))
    for h in range(2):
        ph.append(Phase("proj", 12, 2, 4, name=f"qkv2_{h}", half=h))
    for q in range(4):
        ph.append(Phase("gate", 4, 2, 4, name=f"gates_b{q}", quarter=q))
        ph.append(Phase("branch2s" if q == 3 else "branch2", 4, 4, 1, name=f"mix_b{q}", quarter=q))
    ph.append(Phase("mix", 8, 2, 4, name="w_out2"))
    ph.append(Phase("store", 8, 4, 1, name="ple"))
    for g, n in enumerate((8, 8, 6)):
        ph.append(Phase("upconv", 2 * n, 2, 4, name=f"ffn_up{g}", group=g))
        if g == 2:
            ph.append(Phase("accsq", 8, 4, 3, name="ffn_down2", group=g))
        else:
            ph.append(Phase("store" if g == 0 else "accum", 8, 2, 4, name=f"ffn_down{g}", group=g))
    ph.append(Phase("final", 8, 2, 4, name="ple_gate"))
    piece = unit = 0
    count = {k: 0 for k in ADDS}
    for x in ph:
        assert x.units % x.U == 0 and x.U % 2 == 0 and (x.U * x.ppu) % RING == 0
        x.piece0, x.unit0, x.bodies = piece, unit, x.units // x.U
        x.count0 = dict(count)
        piece += x.units * x.ppu
        unit += x.units
        for k, kinds in ADDS.items():
            count[k] += x.bodies * sum(kinds.get(x.kind, [0])[:x.U])
    return ph


def unit_no(ph, i, j):
    return i * ph.U + (ph.unit0 + j)


def piece_no(ph, i, j, s):
    return i * (ph.U * ph.ppu) + (ph.piece0 + j * ph.ppu + s)


def after(name, ph, i, j):
    adds = ADDS[name][ph.kind][:ph.U]
    return i * sum(adds) + (ph.count0[name] + sum(adds[:j + 1]))


def tiles(buf, at, n=1):
    if isinstance(at, int):
        return buf[:, at:at + n, :]
    return buf[:, bass.ds(at, n), :]


def tile(buf, at):
    return tiles(buf, at).rearrange("p o n -> p (o n)")


def zview(buf, t):
    return buf[:, t:t + 2, :].rearrange("p o n -> p (o n)")[:, 0:3 * P]


def build(nc, A, out):
    PH = plan()
    BY = {x.name: x for x in PH}
    COL, NPAR = param_columns()

    with ExitStack() as ctx:
        def sb(name, shape, dt=F32):
            return ctx.enter_context(nc.sbuf_tensor(name, shape, dt))

        def sem(name):
            return ctx.enter_context(nc.semaphore(name))

        raw = sb("raw", [P, RING, 4 * S])
        wh = sb("w_high", [P, RING, 4 * S], F32R)
        wl = sb("w_low", [P, RING, 4 * S], F32R)
        act_a = sb("act_a", [P, KT, 2 * S], F32R)
        act_b = sb("act_b", [P, KT, 2 * S], F32R)
        G = sb("gates", [P, 32, S])
        PJ = sb("proj", [P, 34, S])
        par = sb("params", [P, NPAR])
        common = sb("common", [P, 2 * P])
        cbuf = sb("small_ops", [P, 2192])
        bcopy = sb("bcopy", [P, 2, 2, S])
        summ = sb("summ", [P, 2, 2, S])
        sqt = sb("sqt", [P, 2, 2, S])
        sqacc = sb("sqacc", [P, 2, S])
        rstd = sb("rstd", [P, S])
        rms_buf = sb("rms", [P, S])
        stat = sb("stat", [P, 64])
        ps = ctx.enter_context(nc.psum_tensor("ps_gemm", [P, 2, 2, 2 * S], F32))
        pm = ctx.enter_context(nc.psum_tensor("ps_small", [P, 4, 2 * S], F32))

        ident, ones = common[:, 0:P], common[:, P:2 * P]
        wr_bd = cbuf[:, 0:512].rearrange("p (c n) -> p c n", c=4)
        wi_bd = cbuf[:, 512:1024].rearrange("p (c n) -> p c n", c=4)
        pool_w = cbuf[:, 1024:1536].rearrange("p (c n) -> p c n", c=4)
        w_f = cbuf[:, 1536:1664].rearrange("p (k n) -> p k n", k=KT)
        same_head = cbuf[:, 1664:1792]
        mask3 = cbuf[:, 1792:2176]
        inv16 = cbuf[:, 2176:2192]
        dist = cbuf[:, 0:768].rearrange("p (g n) -> p g n", g=GROUPS)
        before01 = cbuf[:, 768:1024]
        before_neg = cbuf[:, 1024:1280]
        later = cbuf[:, 1280:1408]
        sel_t = G[0:HEADS, 8:12, :].rearrange("p (h a) n -> p (h a n)", a=2).rearrange("p (h n) -> p h n", h=HEADS)
        onesrow = G[:, 12, :]

        resid = PJ[:, 0:KT, :]
        merged_m = PJ[:, KT:2 * KT, :]

        def pcol(name, i=0):
            c = COL[name]
            if isinstance(i, int):
                return par[:, c + i:c + i + 1]
            return par[:, bass.ds(i + c, 1)]

        raw_full = [sem(f"raw_full{s}") for s in range(RING)]
        high_ready = sem("high_ready")
        split_done = sem("split_done")
        w_used = sem("w_used")
        b_copied = sem("b_copied")
        summed = sem("summed")
        epi_done = sem("epi_done")
        step = {k: sem(k) for k in ADDS}
        scaled, acted, conv_base = step["scaled"], step["acted"], step["conv_base"]
        conv_tap, conv_done = step["conv_tap"], step["conv_done"]
        merged, high_out, squared, sq_added = step["merged"], step["high_out"], step["squared"], step["sq_added"]

        in_par, in_common, in_c1, in_wf, in_c2, in_p, in_resid = (
            sem("in_" + n) for n in ("params", "common", "consts1", "w_f", "consts2", "p", "resid"))
        in_x = [sem(f"in_x{b}") for b in range(4)]
        stored = sem("stored")
        sq0_ready, sq0_added, hi0, lo0 = sem("sq0_ready"), sem("sq0_added"), sem("hi0"), sem("lo0")
        acc_reset, ssq_ready, rms_ready, rstd_ready = (
            sem("acc_reset"), sem("ssq_ready"), sem("rms_ready"), sem("rstd_ready"))
        act_chain, dve_chain, pool_chain = sem("act_chain"), sem("dve_chain"), sem("pool_chain")
        chain = {"act": 0, "dve": 0, "pool": 0}
        act_gate, pool_gate = sem("act_gate"), sem("pool_gate")
        zeroed, bd_zeroed = sem("zeroed"), sem("bd_zeroed")
        y_high, y_done = sem("y_high"), sem("y_done")
        f_logits, f_biased, f_log, cum_ready, cumt_ps, cumt_ready = (
            sem(n) for n in ("f_logits", "f_biased", "f_log", "cum_ready", "cumt_ps", "cumt_ready"))
        nscale_ready, sp_exp = sem("nscale_ready"), sem("sp_exp")
        lru_base, lru_u, lru_ps, lru_act, lru_pre, lru_sqrt, lru_h = (
            sem(n) for n in ("lru_base", "lru_u", "lru_ps", "lru_act", "lru_pre", "lru_sqrt", "lru_h"))
        win_ready, pooled, pool_ps, pool_y = (sem(n) for n in ("win_ready", "pooled", "pool_ps", "pool_y"))
        sc_z, sc_base, sc_y = sem("sc_z"), sem("sc_base"), sem("sc_y")
        at_sq, at_ssq, at_rms, at_qk, at_vps, at_v, at_nc, at_mask = (
            sem(n) for n in ("at_sq", "at_ssq", "at_rms", "at_qk", "at_vps", "at_v", "at_nc", "at_mask"))
        at_lg, at_max, at_exp, at_p, at_pt, at_ptc, at_o = (
            sem(n) for n in ("at_lg", "at_max", "at_exp", "at_p", "at_pt", "at_ptc", "at_o"))
        b_q, b_vps, b_v, b_lg, b_max, b_exp, b_p, b_pt, b_ptc, b_o = (
            sem("b_" + n) for n in ("q", "vps", "v", "lg", "max", "exp", "p", "pt", "ptc", "o"))
        s_z, s_abs, s_ln, s_lnb, s_suf, s_logw, s_w, s_o = (
            sem("s_" + n) for n in ("z", "abs", "ln", "lnb", "suf", "logw", "w", "o"))
        m_high, m_low = sem("m_high"), sem("m_low")
        p_high, p_low = sem("p_high"), sem("p_low")
        pn_t, pn_r, pn_high, pn_low, pn_sq, pn_added = (
            sem("pn_" + n) for n in ("t", "r", "high", "low", "sq", "added"))

        def rows(w):
            return w.rearrange("(t p) n -> p t n", p=P)

        W = {k: rows(A[k]) for k in ("w_in", "w_branch", "w_out", "w_mlp_up", "w_mlp_down", "w_in_2",
                                     "w_branch_a_2", "w_branch_b_2", "w_out_2", "w_up_2", "w_down_2",
                                     "w_ple_in_2", "w_ple_gate_2")}
        x_v = rows(A["x_t"])
        p_v = rows(A["p_t"])
        out_v = rows(out)

        def source(ph, i, j, s):
            u = i * ph.U + j
            n, q = ph.name, ph.quarter
            k0, kn = 4 * s, 4
            if n == "proj":
                w, c = "w_in", u * 256
            elif n.startswith("gates_b"):
                w, c = "w_in_2", i * D + (N_G2 + q * 512 + j * 256)
            elif n.startswith("gates_a"):
                w, c = "w_in", i * D + (N_G + q * 512 + j * 256)
            elif n.startswith("mix_b"):
                w, c = ("w_branch_a_2", "w_branch_b_2")[j % 2], i * 512 + (q * 512 + j // 2 * 256)
            elif n.startswith("mix_a"):
                w, c, k0 = "w_branch", i * 256 + q * 512, 4 * j
            elif n == "w_out":
                w, c = "w_out", u * 256
            elif n == "w_out2":
                w, c = "w_out_2", u * 256
            elif n.startswith("ffn_up"):
                w, c = "w_up_2", i * 256 + (j * DFF2 + ph.group * D)
            elif n.startswith("mlp_up"):
                w, c = "w_mlp_up", u * 256 + ph.group * D
            elif n.startswith("ffn_down"):
                w, c, k0 = "w_down_2", u * 256, 16 * ph.group + 4 * s
            elif n.startswith("mlp_down"):
                w, c, k0 = "w_mlp_down", u * 256, 16 * ph.group + 4 * s
            elif n.startswith("qkv2"):
                w, c = "w_in_2", u * 512 + ph.half * 256
            elif n == "ple":
                w, c, kn = "w_ple_in_2", u * 256, 2
            else:
                w, c = "w_ple_gate_2", u * 256
            cols = slice(c, c + 256) if isinstance(c, int) else bass.ds(c, 256)
            return W[w][:, k0:k0 + kn, cols]

        def slot(ph, j, s):
            return (j * ph.ppu + s) % RING

        def over(eng, body, start, end):
            if end - start > 1:
                with eng.Fori(start, end) as i:
                    body(i)
            elif end > start:
                body(start)

        def skewed(eng, pending, ph, pieces, epilogue, started=False, once=None):
            U, last = ph.U, ph.bodies - 1
            if not started:
                pieces(ph, 0, 0)
            if pending:
                pending()

            def body(i):
                for j in range(U):
                    if j + 1 < U:
                        pieces(ph, i, j + 1)
                    else:
                        pieces(ph, i + 1, 0)
                    if once and isinstance(i, int) and i == 0 and j == 0:
                        once()
                    epilogue(ph, i, j)
            if once:
                assert last > 0
                body(0)
            over(eng, body, 1 if once else 0, last)
            for j in range(U - 1):
                pieces(ph, last, j + 1)
                epilogue(ph, last, j)
            return lambda: epilogue(ph, last, U - 1)

        def end_piece(ph, i, j):
            return piece_no(ph, i, j, ph.ppu - 1) + 1 + RING

        def dst_tile(ph, i, j):
            q = ph.quarter
            if ph.kind == "gate":
                return i * 4 + 2 * j
            if ph.kind.startswith("branch4"):
                return i * 2 + 4 * q
            if ph.kind.startswith("branch2"):
                return 4 * q + 2 * (j // 2)
            if ph.kind == "upconv":
                return i * 2
            return (i * ph.U + j) * 2

        block = ctx.enter_context(nc.Block())

        @block.sync
        def _(sp):
            sp.sem_inc(split_done, RING)
            for b in range(4):
                sp.dma_start(tiles(G, 4 * b, 4), x_v[:, 4 * b:4 * b + 4, :]).then_inc(in_x[b], 16)
            sp.dma_start(par[:], A["params"]).then_inc(in_par, 16)
            sp.dma_start(common[:], A["common"]).then_inc(in_common, 16)
            for ph in PH:
                def body(i, ph=ph):
                    for j in range(ph.U):
                        for s in range(ph.ppu):
                            n, at = piece_no(ph, i, j, s), slot(ph, j, s)
                            src = source(ph, i, j, s)
                            kn = src.shape[1]
                            sp.wait_ge(split_done, n + 1)
                            sp.dma_start(raw[:, at, 0:kn * S].rearrange("p (t n) -> p t n", t=kn),
                                         src).then_inc(raw_full[at], 16)
                over(sp, body, 0, ph.bodies)
            fin = BY["ple_gate"]
            for u in range(8):
                sp.wait_ge(epi_done, fin.unit0 + u + 1 + 2)
                sp.dma_start(out_v[:, 2 * u:2 * u + 2, :], tiles(PJ, 2 * u, 2)).then_inc(stored, 16)
            sp.wait_ge(stored, 8 * 16)

        @block.tensor
        def _(pe):
            pe.sem_inc(w_used, RING)

            def high(t):
                return t[:, 0:S]

            def units(ph, x_in, need=None, once=None):
                def body(i):
                    for j in range(ph.U):
                        n, g = unit_no(ph, i, j), j % 2
                        pe.wait_ge(summed, n + 1)
                        kn = 2 if ph.name == "ple" else 4
                        for s in range(ph.ppu):
                            at = slot(ph, j, s)
                            if need:
                                need(i, j, s)
                            pe.wait_ge(split_done, piece_no(ph, i, j, s) + 1 + RING)
                            for k in range(kn):
                                x = x_in(i, j, 4 * s + k)
                                first = s == 0 and k == 0
                                final = s == ph.ppu - 1 and k == kn - 1
                                for t in range(2):
                                    o = k * S + t * P
                                    nc.tensor.matmul(ps[:, g, t, :], wh[:, at, o:o + P], x,
                                                     start=first, stop=False, skip_group_check=True)
                                    last = nc.tensor.matmul(ps[:, g, t, 0:S], wl[:, at, o:o + P], high(x),
                                                            start=False, stop=final, skip_group_check=True)
                            last.then_inc(w_used, 1)
                        if once and isinstance(i, int) and i == 0 and j == 0:
                            once()
                if once:
                    body(0)
                over(pe, body, 1 if once else 0, ph.bodies)

            def from_buf(buf):
                return lambda i, j, k: buf[:, k, :]

            def ssq(n, ready, value):
                pe.wait_ge(ready, value)
                if n:
                    pe.wait_ge(rms_ready, n)
                nc.tensor.matmul(pm[:, 3, 0:S], ones, sqacc[:, 0, :], start=True, stop=False)
                nc.tensor.matmul(pm[:, 3, 0:S], ones, sqacc[:, 1, :], start=False, stop=True).then_inc(ssq_ready, 1)

            pe.wait_ge(in_common, 16)
            def need_x(i, j, s):
                pe.wait_ge(lo0, 2 * (s + 1))
            units(BY["proj"], from_buf(act_a), need_x, lambda: ssq(0, sq0_added, 8))

            pe.wait_ge(in_wf, 16)
            for k in range(KT):
                for half in range(2):
                    last = nc.tensor.matmul(pm[0:HEADS, 0, 0:S], w_f[:, k, :],
                                            act_a[:, k, half * S:half * S + S].bitcast(F32),
                                            start=(k == 0 and half == 0), stop=(k == KT - 1 and half == 1))
            last.then_inc(f_logits, 1)

            pe.wait_ge(in_c1, 22 * 16)
            for c in range(BT):
                pe.wait_ge(lru_u, 3 * (c + 1))
                if c:
                    pe.wait_ge(lru_act, c)
                nc.tensor.matmul(pm[:, 1, 0:S], wr_bd[:, c, :], tile(G, 16), start=True, stop=True)
                nc.tensor.matmul(pm[:, 1, S:2 * S], wi_bd[:, c, :], tile(G, 16), start=True,
                                 stop=True).then_inc(lru_ps, 1)
                pe.wait_ge(pooled, c + 1)
                if c:
                    pe.wait_ge(pool_y, c)
                nc.tensor.matmul(pm[:, 2, 0:S], pool_w[:, c, :], tile(G, 25), start=True,
                                 stop=True).then_inc(pool_ps, 1)
            pe.wait_ge(cum_ready, 1)
            for q in range(2):
                last = nc.tensor.transpose(pm[:, 0, 256 + 8 * q:264 + 8 * q],
                                           PJ[0:HEADS, 32, q * P:q * P + P], ident[0:HEADS, 0:HEADS])
            last.then_inc(cumt_ps, 1)
            pe.wait_ge(cumt_ready, 1)
            for c in range(BT):
                pe.wait_ge(at_sq, c + 1)
                if c:
                    pe.wait_ge(y_high, 12 + c)
                nc.tensor.matmul(pm[:, 0, :], same_head, G[:, 16:18, :].rearrange("p o n -> p (o n)"),
                                 start=True, stop=True).then_inc(at_ssq, 1)
                if c == 0:
                    pe.wait_ge(lru_act, BT)
                for q in range(2):
                    last = nc.tensor.transpose(pm[:, 1, q * P:q * P + P], PJ[:, 28 + c, q * P:q * P + P], ident)
                last.then_inc(at_vps, 1)
                pe.wait_ge(at_qk, c + 1)
                pe.wait_ge(at_v, c + 1)
                for e in range(2):
                    h = 2 * c + e
                    if h == 0:
                        pe.wait_ge(pool_y, BT)
                    nc.tensor.matmul(pm[:, 1, 0:P], sel_t[:, h, :], PJ[0:HEADS, 33, 0:P],
                                     start=True, stop=True)
                    nc.tensor.matmul(pm[:, 1, P:3 * P], sel_t[:, h, :], PJ[0:HEADS, 33, :],
                                     start=True, stop=True).then_inc(at_nc, 1)
                    qk = slice(HD * e, HD * e + HD)
                    if h:
                        pe.wait_ge(at_ptc, h)
                    nc.tensor.matmul(pm[:, 2, 0:P], G[qk, 20, 0:P], G[qk, 21, 0:P], start=True, stop=True)
                    nc.tensor.matmul(pm[:, 2, P:3 * P], G[qk, 20, P:S], G[qk, 21, :], start=True,
                                     stop=True).then_inc(at_lg, 1)
                    pe.wait_ge(at_p, h + 1)
                    for b in range(3):
                        last = nc.tensor.transpose(pm[:, 2, b * P:b * P + P],
                                                   G[:, 25:27, :].rearrange("p o n -> p (o n)")[:, b * P:b * P + P], ident)
                    last.then_inc(at_pt, 1)
                    pe.wait_ge(at_ptc, h + 1)
                    pt = G[:, 27:29, :].rearrange("p o n -> p (o n)")
                    nc.tensor.matmul(pm[qk, 0, 0:P], G[:, 22, qk], pt[:, 0:P], start=True, stop=True)
                    nc.tensor.matmul(pm[qk, 0, P:S], G[:, 22, qk], pt[:, P:2 * P], start=True, stop=False)
                    last = nc.tensor.matmul(pm[qk, 0, P:S], G[:, 22, P + HD * e:P + HD * e + HD], pt[:, 2 * P:3 * P],
                                            start=False, stop=True)
                last.then_inc(at_o, 1)

            for q in range(4):
                units(BY[f"gates_a{q}"], from_buf(act_a))

                def need_y(i, j, s):
                    pe.wait_ge(y_done, 16)
                units(BY[f"mix_a{q}"], lambda i, j, k: act_b[:, 4 * j + k, :], need_y)

            def after_phase(name, extra=None):
                src = BY[name]

                def need(i, j, s):
                    done = (src.unit0 + min(src.units, 2 * (s + 1))) if src.kind != "upconv" else (
                        src.unit0 + min(src.units, 4 * (s + 1)))
                    if extra:
                        extra(s)
                    pe.wait_ge(epi_done, done + 2)
                return need

            def need_m(i, j, s):
                if s < 3:
                    pe.wait_ge(m_low, 4 * (s + 1))
                else:
                    pe.wait_ge(epi_done, BY["mix_a3"].unit0 + 8 + 2)
            units(BY["w_out"], from_buf(act_a), need_m)
            for g in range(4):
                if g == 0:
                    units(BY["mlp_up0"], from_buf(act_b), after_phase("w_out"),
                          lambda: ssq(1, sq_added, BY["w_out"].count0["sq_added"] + 8 + 2))
                else:
                    units(BY[f"mlp_up{g}"], from_buf(act_b))
                units(BY[f"mlp_down{g}"], from_buf(act_a), after_phase(f"mlp_up{g}"))

            units(BY["qkv2_0"], from_buf(act_b), after_phase("mlp_down3"),
                  lambda: ssq(2, sq_added, BY["mlp_down3"].count0["sq_added"] + 8 + 2))
            for half in range(2):
                if half:
                    units(BY["qkv2_1"], from_buf(act_b))
                if half == 0:
                    pe.wait_ge(in_c2, 16)
                for e in range(2):
                    h = 2 * half + e
                    pe.wait_ge(b_q, h + 1)
                    if h:
                        pe.wait_ge(y_high, 16 + 4 * half + e)
                        pe.wait_ge(b_ptc, 2 * h)
                    for g in range(GROUPS):
                        for q in range(2):
                            last = nc.tensor.transpose(
                                pm[:, g // 2, (g % 2) * S + q * P:(g % 2) * S + q * P + P],
                                G[:, 12 + 2 * g + e, q * P:q * P + P], ident)
                    last.then_inc(b_vps, 1)
                    pe.wait_ge(b_v, h + 1)
                    for q in range(2):
                        n = 2 * h + q
                        kw = P * (q + 1)
                        for g in range(GROUPS):
                            last = nc.tensor.matmul(pm[:, g // 2, (g % 2) * S:(g % 2) * S + kw],
                                                    PJ[:, 16 + g, q * P:q * P + P],
                                                    G[:, 6 + 2 * g + e, 0:kw], start=True, stop=True)
                        last.then_inc(b_lg, 1)
                        pe.wait_ge(b_p, n + 1)
                        for b in range(GROUPS * (q + 1)):
                            g, kt = b // (q + 1), b % (q + 1)
                            last = nc.tensor.transpose(pm[:, g // 2, (g % 2) * S + kt * P:(g % 2) * S + kt * P + P],
                                                       PJ[:, 19 + g, kt * P:kt * P + P], ident)
                        last.then_inc(b_pt, 1)
                        pe.wait_ge(b_ptc, n + 1)
                        nb = GROUPS * (q + 1)
                        for b in range(nb):
                            g, kt = b // (q + 1), b % (q + 1)
                            last = nc.tensor.matmul(pm[:, 2, q * P:q * P + P],
                                                    PJ[:, 25 + g, kt * P:kt * P + P],
                                                    PJ[:, 22 + g, kt * P:kt * P + P],
                                                    start=(b == 0), stop=(b == nb - 1))
                    last.then_inc(b_o, 1)
                for e in range(2):
                    h = 2 * half + e
                    if e == 0:
                        pe.wait_ge(y_high, 16 + 4 * half + 2)
                    else:
                        pe.wait_ge(y_high, 16 + 4 * half + 3)
                    for q in range(2):
                        last = nc.tensor.transpose(pm[:, 2, q * P:q * P + P], G[:, 22 + e, q * P:q * P + P], ident)
                    last.then_inc(s_z, 1)
                    pe.wait_ge(s_abs, 2 * h + 1)
                    nc.tensor.matmul(pm[:, 0, 0:S], G[:, 20 + e, 0:P], PJ[:, 16, :], start=True, stop=True)
                    nc.tensor.matmul(pm[:, 0, S:S + P], G[:, 20 + e, P:S], PJ[:, 16, P:S], start=True,
                                     stop=True).then_inc(s_z, 1)
                    pe.wait_ge(s_ln, h + 1)
                    nc.tensor.matmul(pm[:, 1, 0:S], later, PJ[:, 18, :], start=True, stop=False,
                                     skip_group_check=True)
                    nc.tensor.matmul(pm[:, 1, P:S], ones, PJ[:, 19, 0:P], start=False, stop=True,
                                     skip_group_check=True)
                    nc.tensor.matmul(pm[:, 1, S:S + P], later, PJ[:, 19, 0:P], start=True, stop=True,
                                     skip_group_check=True).then_inc(s_suf, 1)
                    pe.wait_ge(s_w, h + 1)
                    nc.tensor.matmul(pm[:, 2, 0:S], PJ[:, 17, 0:P], PJ[:, 22, :], start=True, stop=False,
                                     skip_group_check=True)
                    nc.tensor.matmul(pm[:, 2, P:S], PJ[:, 17, P:S], PJ[:, 23, 0:P], start=False, stop=True,
                                     skip_group_check=True).then_inc(s_o, 1)

            for q in range(4):
                units(BY[f"gates_b{q}"], from_buf(act_b))

                def need_y2(i, j, s):
                    pe.wait_ge(y_done, 24)
                units(BY[f"mix_b{q}"], lambda i, j, k: act_a[:, 4 * (j % 2) + k, :], need_y2)

            def need_m2(i, j, s):
                if s < 3:
                    pe.wait_ge(m_low, 12 + 4 * (s + 1))
                else:
                    pe.wait_ge(epi_done, BY["mix_b3"].unit0 + 4 + 2)
            units(BY["w_out2"], from_buf(act_b), need_m2)

            def need_p(i, j, s):
                pe.wait_ge(p_low, 1)
            units(BY["ple"], from_buf(act_b), need_p)
            ssq(3, sq_added, BY["w_out2"].count0["sq_added"] + 8 + 2)

            def need_pn(first):
                def need(i, j, s):
                    pe.wait_ge(pn_low, first + 4 * (s + 1))
                return need
            for g in range(3):
                if g == 0:
                    units(BY["ffn_up0"], from_buf(act_a), need_pn(0), lambda: ssq(4, pn_added, 8))
                else:
                    units(BY[f"ffn_up{g}"], from_buf(act_a))
                units(BY[f"ffn_down{g}"], from_buf(act_b), after_phase(f"ffn_up{g}"))
            ssq(5, sq_added, BY["ffn_down2"].count0["sq_added"] + 8 + 2)
            units(BY["ple_gate"], from_buf(act_a), need_pn(16))

        @block.scalar
        def _(act):
            def link(ins):
                chain["act"] += 1
                ins.then_inc(act_chain, 1)
                act.wait_ge(act_chain, chain["act"])

            def pieces(ph, i, j):
                kn = 2 if ph.name == "ple" else 4
                for s in range(ph.ppu):
                    n, at = piece_no(ph, i, j, s), slot(ph, j, s)
                    body_rounds = ph.U * ph.ppu // RING
                    rnd = i * body_rounds + (ph.piece0 + j * ph.ppu + s) // RING + 1
                    act.wait_ge(raw_full[at], rnd * 16)
                    act.wait_ge(w_used, n + 1)
                    nc.scalar.copy(wh[:, at, 0:kn * S], raw[:, at, 0:kn * S]).then_inc(high_ready, 1)

            def apart():
                act.sem_inc(act_gate, 1)

            def epilogue(ph, i, j):
                k, g, n = ph.kind, j % 2, unit_no(ph, i, j)
                act.wait_ge(w_used, end_piece(ph, i, j))
                act.wait_ge(summed, n + 1)
                nc.scalar.copy(bcopy[:, g], ps[:, g, :, S:2 * S]).then_inc(b_copied, 1)
                t0 = dst_tile(ph, i, j)
                if k == "gate":
                    act.wait_ge(scaled, after("scaled", ph, i, j))
                    act.wait_ge(epi_done, n + 2)
                    apart()
                    nc.scalar.activation(tiles(G, t0, 2), summ[:, g], ACT.Sigmoid).then_inc(epi_done, 1)
                elif (k == "branch4s" and j == 3) or (k == "branch2s" and j % 2 == 1):
                    buf = act_a if k == "branch4s" else act_b
                    act.wait_ge(merged, after("merged", ph, i, j))
                    apart()
                    nc.scalar.copy(tiles(buf, t0, 2)[:, :, 0:S], tiles(PJ, t0 + 16, 2)).then_inc(high_out, 1)
                elif k == "resid":
                    gain = "g_mlp" if ph.name == "w_out" else "g_mix_pre2"
                    act.wait_ge(merged, after("merged", ph, i, j))
                    apart()
                    for t in range(2):
                        last = nc.scalar.activation(tile(act_b, t0 + t)[:, 0:S], tile(PJ, t0 + t), ACT.Copy,
                                                    scale=pcol(gain, t0 + t))
                    last.then_inc(high_out, 1)
                    square(tiles(PJ, t0, 2), g, after("squared", ph, i, j))
                elif k == "up":
                    act.wait_ge(acted, after("acted", ph, i, j))
                    apart()
                    nc.scalar.copy(tiles(act_a, t0, 2)[:, :, 0:S], summ[:, g]).then_inc(high_out, 1)
                elif k in ("mix", "accsq"):
                    if k == "mix":
                        act.wait_ge(epi_done, n + 1 + 2)
                    else:
                        act.wait_ge(merged, after("merged", ph, i, j))
                    square(tiles(PJ, t0 + 16, 2), g, after("squared", ph, i, j))
                elif k == "upconv":
                    act.wait_ge(scaled, after("scaled", ph, i, j))
                    if j == 0:
                        act.wait_ge(epi_done, n + 2)
                    c0 = i * 2 + (16 * ph.group + 44 * j)
                    apart()
                    for t in range(2):
                        last = nc.scalar.activation(G[:, 28 + 2 * j + t, :], summ[:, g, t], ACT.Identity,
                                                    scale=pcol("conv_w2", c0 + t + 176), bias=pcol("conv_b2", c0 + t))
                    last.then_inc(conv_base, 1)
                    act.wait_ge(acted, after("acted", ph, i, j))
                    if j == 0:
                        act.wait_ge(epi_done, n + 2)
                        nc.scalar.activation(G[:, 28:30, :], G[:, 28:30, :], ACT.Gelu_apprx_tanh).then_inc(epi_done, 1)
                    else:
                        apart()
                        nc.scalar.copy(tiles(act_b, t0, 2)[:, :, 0:S], G[:, 30:32, :]).then_inc(high_out, 1)
                elif k == "final":
                    act.wait_ge(summed, n + 1 + 2)
                    nc.scalar.activation(summ[:, g], summ[:, g], ACT.Sigmoid).then_inc(acted, 1)

            def square(src, g, value):
                act.wait_ge(sq_added, value)
                apart()
                nc.scalar.activation(sqt[:, g], src, ACT.Square).then_inc(squared, 1)

            def rms(n):
                act.wait_ge(ssq_ready, n + 1)
                if n:
                    act.wait_ge(rstd_ready, n)
                nc.scalar.activation(rms_t, pm[:, 3, 0:S], ACT.Sqrt, scale=1.0 / D, bias=eps_t).then_inc(rms_ready, 1)

            rms_t = rms_buf[:]
            eps_t = stat[:, 63:64]

            act.wait_ge(in_par, 16)
            for b in range(8):
                act.wait_ge(in_x[b // 2], 16)
                if b >= 2:
                    act.wait_ge(sq0_added, b - 1)
                nc.scalar.activation(sqt[:, b % 2], tiles(G, 2 * b, 2), ACT.Square).then_inc(sq0_ready, 1)
                for t in range(2):
                    last = nc.scalar.activation(act_a[:, 2 * b + t, 0:S], G[:, 2 * b + t, :], ACT.Copy,
                                                scale=pcol("g_mix", 2 * b + t))
                last.then_inc(hi0, 1)
            act.wait_ge(zeroed, 1)
            pend = None
            pend = skewed(act, None, BY["proj"], pieces, epilogue, once=lambda: rms(0))
            pieces(BY["gates_a0"], 0, 0)
            pend()

            lam = par[:, COL["lru_lambda"]:COL["lru_lambda"] + 4]
            link(nc.scalar.activation(stat[:, 0:4], lam, ACT.Abs))
            link(nc.scalar.activation(stat[:, 4:8], stat[:, 0:4], ACT.Exp, scale=-1.0))
            nc.scalar.activation(stat[:, 8:12], stat[:, 4:8], ACT.Ln, bias=1.0).then_inc(sp_exp, 1)
            act.wait_ge(f_biased, 1)
            link(nc.scalar.activation(G[0:HEADS, 30, :], PJ[0:HEADS, 32, :], ACT.Abs))
            link(nc.scalar.activation(G[0:HEADS, 30, :], G[0:HEADS, 30, :], ACT.Exp, scale=-1.0))
            nc.scalar.activation(G[0:HEADS, 30, :], G[0:HEADS, 30, :], ACT.Ln, bias=1.0).then_inc(f_log, 1)
            act.wait_ge(nscale_ready, 1)
            for c in range(BT):
                if c:
                    act.wait_ge(y_done, 3 * c)
                nc.scalar.activation(tile(G, 16), PJ[:, c, :], ACT.Identity, scale=pcol("lru_conv_w", 12 + c),
                                     bias=pcol("lru_conv_b", c)).then_inc(lru_base, 1)
                act.wait_ge(sc_z, c + 1)
                nc.scalar.activation(tile(G, 28), tile(G, 27), ACT.Copy,
                                     scale=pcol("sconv_w", 8 + c)).then_inc(sc_base, 1)
                act.wait_ge(lru_ps, c + 1)
                nc.scalar.activation(tile(G, 17), pm[:, 1, 0:S], ACT.Sigmoid, bias=pcol("lru_br", c))
                nc.scalar.activation(tile(G, 18), pm[:, 1, S:2 * S], ACT.Sigmoid,
                                     bias=pcol("lru_bi", c)).then_inc(lru_act, 1)
                act.wait_ge(lru_act, c + 1)
                nc.scalar.activation(tile(G, 19), tile(G, 17), ACT.Exp, scale=stat[:, 12 + c:13 + c])
                nc.scalar.activation(tile(G, 20), tile(G, 17), ACT.Tanh,
                                     scale=stat[:, 12 + c:13 + c]).then_inc(lru_pre, 1)
                act.wait_ge(pool_ps, c + 1)
                nc.scalar.activation(tile(G, 26), pm[:, 2, 0:S], ACT.Copy,
                                     scale=pcol("pool_scale", c)).then_inc(pool_y, 1)
                act.wait_ge(lru_sqrt, 2 * c + 1)
                nc.scalar.activation(tile(G, 21), tile(G, 21), ACT.Sqrt).then_inc(lru_sqrt, 1)
                act.wait_ge(lru_h, c + 1)
                nc.scalar.copy(act_b[:, c, 0:S], tile(G, 22)).then_inc(y_high, 1)
                act.wait_ge(pool_y, c + 1)
                nc.scalar.copy(act_b[:, 4 + c, 0:S], tile(G, 26)).then_inc(y_high, 1)
                act.wait_ge(sc_y, c + 1)
                nc.scalar.copy(act_b[:, 8 + c, 0:S], tile(G, 28)).then_inc(y_high, 1)
            act.wait_ge(y_done, 12)
            for c in range(BT):
                nc.scalar.activation(G[:, 16, :], PJ[:, 20 + c, :], ACT.Square)
                nc.scalar.activation(G[:, 17, :], PJ[:, 24 + c, :], ACT.Square).then_inc(at_sq, 1)
                act.wait_ge(at_ssq, c + 1)
                if c:
                    act.wait_ge(at_qk, c)
                nc.scalar.activation(G[:, 18:20, :].rearrange("p o n -> p (o n)"), pm[:, 0, :], ACT.Sqrt,
                                     scale=1.0 / HD, bias=eps_t).then_inc(at_rms, 1)
                for e in range(2):
                    h = 2 * c + e
                    act.wait_ge(at_max, h + 1)
                    sv = G[:, 25:27, :].rearrange("p o n -> p (o n)")
                    nc.scalar.activation(sv[:, 0:P], sv[:, 0:P], ACT.Exp, bias=stat[:, 34:35],
                                         accum_out=stat[:, 36:37])
                    nc.scalar.activation(sv[:, P:3 * P], sv[:, P:3 * P], ACT.Exp, bias=stat[:, 35:36],
                                         accum_out=stat[:, 37:38]).then_inc(at_exp, 1)
                act.wait_ge(at_o, c + 1)
                if c:
                    act.wait_ge(y_done, 12 + c)
                nc.scalar.copy(G[:, 29, :], pm[:, 0, 0:S]).then_inc(act_chain, 1)
                chain["act"] += 1
                act.wait_ge(act_chain, chain["act"])
                nc.scalar.copy(act_b[:, 12 + c, 0:S], G[:, 29, :]).then_inc(y_high, 1)

            def phases(names, pend):
                for n in names:
                    pend = skewed(act, pend, BY[n], pieces, epilogue)
                return pend

            def merge_phases(gname, bname, buf):
                pend = skip_first(BY[gname + "0"])
                pend = phases([bname + "0", gname + "1", bname + "1", gname + "2", bname + "2", gname + "3"], pend)
                last = BY[gname + "3"]
                pieces(BY[bname + "3"], 0, 0)
                pend()
                act.wait_ge(w_used, end_piece(last, last.bodies - 1, last.U - 1))
                for t in range(12):
                    nc.scalar.copy(buf[:, t, 0:S], PJ[:, 16 + t, :]).then_inc(m_high, 1)
                return skip_first(BY[bname + "3"])

            def skip_first(ph, once=None):
                return skewed(act, None, ph, pieces, epilogue, True, once)

            pend = merge_phases("gates_a", "mix_a", act_a)
            pend = phases(["w_out"], pend)
            pieces(BY["mlp_up0"], 0, 0)
            pend()
            pend = skip_first(BY["mlp_up0"], lambda: rms(1))
            pend = phases(["mlp_down0", "mlp_up1", "mlp_down1", "mlp_up2", "mlp_down2", "mlp_up3", "mlp_down3"], pend)
            pieces(BY["qkv2_0"], 0, 0)
            pend()
            pend = skip_first(BY["qkv2_0"], lambda: rms(2))
            for half in range(2):
                pieces(BY["qkv2_1" if half == 0 else "gates_b0"], 0, 0)
                pend()
                for e in range(2):
                    h = 2 * half + e
                    for q in range(2):
                        n = 2 * h + q
                        act.wait_ge(b_max, n + 1)
                        kw = P * (q + 1)
                        nc.scalar.activation(PJ[:, 19:22, 0:kw], PJ[:, 19:22, 0:kw], ACT.Exp, bias=stat[:, 41:42],
                                             accum_out=stat[:, 42:43]).then_inc(b_exp, 1)
                    act.wait_ge(b_o, h + 1)
                    if h:
                        act.wait_ge(y_done, 16 + 4 * half + e)
                    link(nc.scalar.copy(PJ[:, 30, :], pm[:, 2, 0:S]))
                    nc.scalar.copy(act_a[:, h, 0:S], PJ[:, 30, :]).then_inc(y_high, 1)
                for e in range(2):
                    h = 2 * half + e
                    act.wait_ge(s_abs, 2 * h + 2)
                    z3 = zview(PJ, 20)
                    l3 = zview(PJ, 18)
                    link(nc.scalar.activation(l3, z3, ACT.Abs))
                    link(nc.scalar.activation(l3, l3, ACT.Exp, scale=-1.0))
                    nc.scalar.activation(l3, l3, ACT.Ln, bias=1.0).then_inc(s_lnb, 1)
                    act.wait_ge(s_logw, h + 1)
                    w3 = zview(PJ, 22)
                    nc.scalar.activation(w3, w3, ACT.Exp).then_inc(s_w, 1)
                    act.wait_ge(s_o, h + 1)
                    act.wait_ge(y_done, 16 + 4 * half + 2 + e)
                    link(nc.scalar.copy(PJ[:, 30, :], pm[:, 2, 0:S]))
                    nc.scalar.copy(act_a[:, 4 + h, 0:S], PJ[:, 30, :]).then_inc(y_high, 1)
                if half == 0:
                    pend = skip_first(BY["qkv2_1"])
            pend = merge_phases("gates_b", "mix_b", act_b)
            pend = phases(["w_out2"], pend)
            pieces(BY["ple"], 0, 0)
            pend()
            last = BY["w_out2"]
            act.wait_ge(in_p, 16)
            act.wait_ge(w_used, end_piece(last, last.bodies - 1, last.U - 1))
            nc.scalar.copy(act_b[:, 0:2, 0:S], PJ[:, 32:34, :]).then_inc(p_high, 1)
            pend = skip_first(BY["ple"])
            pieces(BY["ffn_up0"], 0, 0)
            pend()

            def post_norm(n, first, gain, squares):
                rms(n)
                for b in range(8):
                    act.wait_ge(pn_r, first // 2 + b + 1)
                    for t in range(2):
                        k = 2 * b + t
                        if gain:
                            nc.scalar.activation(act_a[:, k, 0:S], PJ[:, k, :], ACT.Copy,
                                                 scale=pcol(gain, k)).then_inc(pn_high, 1)
                        else:
                            nc.scalar.copy(act_a[:, k, 0:S], PJ[:, k, :]).then_inc(pn_high, 1)
                    if squares:
                        if b >= 2:
                            act.wait_ge(pn_added, b - 1)
                        nc.scalar.activation(sqt[:, b % 2], PJ[:, 2 * b:2 * b + 2, :], ACT.Square).then_inc(pn_sq, 1)
            post_norm(3, 0, "g_ffn_pre2", True)
            pend = skip_first(BY["ffn_up0"], lambda: rms(4))
            pend = phases(["ffn_down0", "ffn_up1", "ffn_down1", "ffn_up2", "ffn_down2"], pend)
            pieces(BY["ple_gate"], 0, 0)
            pend()
            post_norm(5, 16, None, False)
            pend = skip_first(BY["ple_gate"])
            pend()

        @block.vector
        def _(dve):
            def link(ins):
                chain["dve"] += 1
                ins.then_inc(dve_chain, 1)
                dve.wait_ge(dve_chain, chain["dve"])

            def pieces(ph, i, j):
                kn = 2 if ph.name == "ple" else 4
                for s in range(ph.ppu):
                    n, at = piece_no(ph, i, j, s), slot(ph, j, s)
                    dve.wait_ge(high_ready, n + 1)
                    nc.vector.tensor_tensor(wl[:, at, 0:kn * S], raw[:, at, 0:kn * S],
                                            wh[:, at, 0:kn * S].bitcast(F32),
                                            ALU.subtract).then_inc(split_done, 1)

            def low(dst, src, inc):
                nc.vector.tensor_tensor(dst[:, :, S:2 * S], src, dst[:, :, 0:S].bitcast(F32), ALU.subtract).then_inc(inc, 1)

            def epilogue(ph, i, j):
                k, g, n = ph.kind, j % 2, unit_no(ph, i, j)
                t0 = dst_tile(ph, i, j)
                A_half = ps[:, g, :, 0:S]
                s2 = summ[:, g]
                dve.wait_ge(b_copied, n + 1)
                dve.wait_ge(epi_done, n + 1)
                if k in ("mix", "store"):
                    dst = tiles(G, t0, 2) if ph.name == "ple" else tiles(PJ, t0 + 16, 2)
                    nc.vector.tensor_tensor(dst, A_half, bcopy[:, g], ALU.add).then_inc(summed, 1)
                    dve.wait_ge(summed, n + 1 + 2)
                    dve.wait_ge(epi_done, n + 2)
                    dve.sem_inc(epi_done, 1)
                    return
                nc.vector.tensor_tensor(s2, A_half, bcopy[:, g], ALU.add).then_inc(summed, 1)
                if k in ("proj", "gate", "up", "upconv"):
                    dve.wait_ge(summed, n + 1 + 2)
                    r2 = rstd[:].unsqueeze(1).to_broadcast([P, 2, S])
                    if k == "proj":
                        dst = tiles(PJ, t0, 2) if ph.name == "proj" else tiles(G, t0, 2)
                        dve.wait_ge(epi_done, n + 2)
                        nc.vector.tensor_tensor(dst, s2, r2, ALU.mult).then_inc(epi_done, 1)
                        return
                    nc.vector.tensor_tensor(s2, s2, r2, ALU.mult).then_inc(scaled, 1)
                if k.startswith("branch"):
                    nb = 4 if k.startswith("branch4") else 2
                    br = j % nb
                    gate = tiles(G, i * 2 + 4 * br, 2) if nb == 4 else tiles(G, 4 * br + 2 * (j // 2), 2)
                    dve.wait_ge(summed, n + 1 + 2)
                    if br == 0:
                        dve.wait_ge(epi_done, n + 2)
                        nc.vector.tensor_tensor(tiles(PJ, t0 + 16, 2), s2, gate, ALU.mult).then_inc(epi_done, 1)
                    else:
                        nc.vector.tensor_tensor(s2, s2, gate, ALU.mult).then_inc(scaled, 1)
                        if br == nb - 1 and k.endswith("s"):
                            dve.wait_ge(high_out, after("high_out", ph, i, j))
                            low(tiles(act_a if nb == 4 else act_b, t0, 2), tiles(PJ, t0 + 16, 2), epi_done)
                elif k == "resid":
                    gain = "g_mlp" if ph.name == "w_out" else "g_mix_pre2"
                    dve.wait_ge(high_out, after("high_out", ph, i, j))
                    dve.wait_ge(epi_done, n + 2)
                    for t in range(2):
                        d = tile(act_b, t0 + t)
                        last = nc.vector.scalar_tensor_tensor(out=d[:, S:2 * S], in0=tile(PJ, t0 + t),
                                                              scalar=pcol(gain, t0 + t), in1=d[:, 0:S].bitcast(F32),
                                                              op0=ALU.mult, op1=ALU.subtract)
                    last.then_inc(epi_done, 1)
                elif k == "up":
                    dve.wait_ge(scaled, after("scaled", ph, i, j))
                    nc.vector.scalar_tensor_tensor(out=s2, in0=s2, scalar=0.0, in1=s2, op0=ALU.max,
                                                   op1=ALU.mult).then_inc(acted, 1)
                    dve.wait_ge(high_out, after("high_out", ph, i, j))
                    dve.wait_ge(epi_done, n + 2)
                    low(tiles(act_a, t0, 2), s2, epi_done)
                elif k == "upconv":
                    dve.wait_ge(conv_base, after("conv_base", ph, i, j))
                    c0 = i * 2 + (16 * ph.group + 44 * j)
                    y = G[:, 28 + 2 * j:30 + 2 * j, :]
                    for tap in (1, 0):
                        sh = 2 - tap
                        for t in range(2):
                            last = nc.vector.scalar_tensor_tensor(
                                out=y[:, t, sh:S], in0=summ[:, g, t, 0:S - sh],
                                scalar=pcol("conv_w2", c0 + t + 88 * tap), in1=y[:, t, sh:S],
                                op0=ALU.mult, op1=ALU.add)
                            if tap:
                                last.then_inc(conv_tap, 1)
                        if tap:
                            dve.wait_ge(conv_tap, after("conv_tap", ph, i, j))
                    if j == 0:
                        last.then_inc(acted, 1)
                    else:
                        last.then_inc(conv_done, 1)
                        dve.wait_ge(conv_done, after("conv_done", ph, i, j))
                        dve.wait_ge(epi_done, n + 2)
                        nc.vector.tensor_tensor(G[:, 30:32, :], G[:, 28:30, :], G[:, 30:32, :],
                                                ALU.mult).then_inc(acted, 1)
                        dve.wait_ge(high_out, after("high_out", ph, i, j))
                        low(tiles(act_b, t0, 2), G[:, 30:32, :], epi_done)
                elif k == "final":
                    dve.wait_ge(acted, after("acted", ph, i, j))
                    nc.vector.tensor_tensor(s2, s2, tiles(G, t0, 2), ALU.mult).then_inc(scaled, 1)

            def recip(n):
                dve.wait_ge(rms_ready, n + 1)
                nc.vector.reciprocal(rstd[:], rms_buf[:]).then_inc(rstd_ready, 1)
                dve.wait_ge(rstd_ready, n + 1)

            dve.sem_inc(summed, 2)
            dve.sem_inc(epi_done, 2)
            nc.vector.memset(stat[:, 63:64], EPS).then_inc(zeroed, 1)
            
            dve.wait_ge(in_par, 16)
            for b in range(8):
                dve.wait_ge(hi0, b + 1)
                for t in range(2):
                    k = 2 * b + t
                    last = nc.vector.scalar_tensor_tensor(out=act_a[:, k, S:2 * S], in0=G[:, k, :],
                                                          scalar=pcol("g_mix", k), in1=act_a[:, k, 0:S].bitcast(F32),
                                                          op0=ALU.mult, op1=ALU.subtract)
                last.then_inc(lo0, 1)

            def skip_first(ph, once=None):
                return skewed(dve, None, ph, pieces, epilogue, True, once)

            def phases(names, pend):
                for n in names:
                    pend = skewed(dve, pend, BY[n], pieces, epilogue)
                return pend

            pend = skewed(dve, None, BY["proj"], pieces, epilogue, once=lambda: recip(0))
            pieces(BY["gates_a0"], 0, 0)
            pend()
            dve.wait_ge(epi_done, BY["gates_a0"].unit0 + 2)

            dve.wait_ge(in_c1, 22 * 16)
            link(nc.vector.memset(onesrow, 1.0))
            lam = par[:, COL["lru_lambda"]:COL["lru_lambda"] + 4]
            link(nc.vector.tensor_scalar(stat[:, 16:20], lam, -1.0, 0.0, ALU.mult, ALU.max))
            dve.wait_ge(sp_exp, 1)
            link(nc.vector.tensor_tensor(stat[:, 16:20], stat[:, 16:20], stat[:, 8:12], ALU.add))
            nc.vector.tensor_scalar(stat[:, 12:16], stat[:, 16:20], -8.0, None, ALU.mult)
            nc.vector.tensor_scalar(stat[:, 20:21], pcol("q_g"), HD ** -0.5, None, ALU.mult).then_inc(nscale_ready, 1)
            dve.wait_ge(f_logits, 1)
            link(nc.vector.tensor_tensor(PJ[0:HEADS, 32, :], pm[0:HEADS, 0, 0:S], rstd[0:HEADS, :], ALU.mult))
            nc.vector.tensor_scalar(PJ[0:HEADS, 32, :], PJ[0:HEADS, 32, :], par[0:HEADS, COL["forget_b"]:COL["forget_b"] + 1],
                                    None, ALU.add).then_inc(f_biased, 1)
            dve.wait_ge(f_log, 1)
            link(nc.vector.scalar_tensor_tensor(out=G[0:HEADS, 31, :], in0=PJ[0:HEADS, 32, :], scalar=0.0,
                                                in1=G[0:HEADS, 30, :], op0=ALU.min, op1=ALU.subtract))
            link(nc.vector.tensor_tensor_scan(PJ[0:HEADS, 32, :], G[0:HEADS, 12, :], G[0:HEADS, 31, :], 0.0,
                                              ALU.mult, ALU.add))
            nc.vector.tensor_scalar(PJ[0:HEADS, 33, :], PJ[0:HEADS, 32, :], -1.0, None, ALU.mult).then_inc(cum_ready, 1)

            for c in range(BT):
                xa = PJ[:, c, :]
                if c:
                    dve.wait_ge(y_done, 3 * c)
                link(nc.vector.tensor_tensor(tile(G, 27), PJ[:, 12 + c, :], PJ[:, 16 + c, :], ALU.mult))
                dve.sem_inc(sc_z, 1)
                u = tile(G, 16)
                dve.wait_ge(lru_base, c + 1)
                for tap in (2, 1, 0):
                    sh = 3 - tap
                    nc.vector.scalar_tensor_tensor(out=u[:, sh:S], in0=xa[:, 0:S - sh],
                                                   scalar=pcol("lru_conv_w", 4 * tap + c), in1=u[:, sh:S],
                                                   op0=ALU.mult, op1=ALU.add).then_inc(lru_u, 1)
                    dve.wait_ge(lru_u, 3 * c + 3 - tap)
                dve.wait_ge(win_ready, c + 1)
                win = 2 << c
                src = tile(G, 23 + c % 2)
                xp = PJ[:, 4 + c, :]
                pw = tile(G, 25)
                link(nc.vector.scalar_tensor_tensor(out=pw, in0=src, scalar=1.0 / win, in1=xp, op0=ALU.mult,
                                                    op1=ALU.subtract))
                link(nc.vector.tensor_tensor(stat[:, 44:44 + win], src[:, 0:win], inv16[:, 0:win], ALU.mult))
                nc.vector.tensor_tensor(pw[:, 0:win], stat[:, 44:44 + win], xp[:, 0:win],
                                        ALU.subtract).then_inc(pooled, 1)
                y = tile(G, 28)
                z = tile(G, 27)
                dve.wait_ge(sc_base, c + 1)
                for tap in (1, 0):
                    sh = 2 - tap
                    link(nc.vector.scalar_tensor_tensor(out=y[:, sh:S], in0=z[:, 0:S - sh],
                                                        scalar=pcol("sconv_w", 4 * tap + c), in1=y[:, sh:S],
                                                        op0=ALU.mult, op1=ALU.add))
                nc.vector.tensor_tensor(y, y, PJ[:, 8 + c, :], ALU.mult).then_inc(sc_y, 1)
                dve.wait_ge(lru_pre, c + 1)
                v = tile(G, 21)
                link(nc.vector.tensor_tensor(v, tile(G, 19), tile(G, 19), ALU.mult))
                link(nc.vector.scalar_tensor_tensor(out=v, in0=v, scalar=1.0, in1=tile(G, 20), op0=ALU.add,
                                                    op1=ALU.mult))
                nc.vector.tensor_scalar(v, v, -1.0, TINY, ALU.mult, ALU.max).then_inc(lru_sqrt, 1)
                link(nc.vector.tensor_tensor(tile(G, 18), tile(G, 18), u, ALU.mult))
                dve.wait_ge(lru_sqrt, 2 * c + 2)
                link(nc.vector.tensor_tensor(v, v, tile(G, 18), ALU.mult))
                nc.vector.tensor_tensor_scan(tile(G, 22), tile(G, 19), v, 0.0, ALU.mult,
                                             ALU.add).then_inc(lru_h, 1)
                for b, src in ((0, 22), (1, 26), (2, 28)):
                    dve.wait_ge(y_high, 3 * c + b + 1)
                    low(act_b[:, 4 * b + c:4 * b + c + 1, :], G[:, src:src + 1, :], y_done)
            dve.wait_ge(cumt_ps, 1)
            nc.vector.tensor_copy(stat[:, 44:60], pm[:, 0, 256:272]).then_inc(cumt_ready, 1)
            dve.wait_ge(cumt_ready, 1)
            dve.wait_ge(y_done, 12)
            for c in range(BT):
                dve.wait_ge(at_rms, c + 1)
                rr = G[:, 18:20, :].rearrange("p o n -> p (o n)")
                link(nc.vector.reciprocal(rr, rr))
                nc.vector.scalar_tensor_tensor(out=G[:, 20, :], in0=PJ[:, 20 + c, :], scalar=stat[:, 20:21],
                                               in1=G[:, 18, :], op0=ALU.mult, op1=ALU.mult)
                nc.vector.scalar_tensor_tensor(out=G[:, 21, :], in0=PJ[:, 24 + c, :], scalar=pcol("k_g"),
                                               in1=G[:, 19, :], op0=ALU.mult, op1=ALU.mult).then_inc(at_qk, 1)
                dve.wait_ge(at_vps, c + 1)
                nc.vector.tensor_copy(G[:, 22, :], pm[:, 1, 0:S]).then_inc(at_v, 1)
                for e in range(2):
                    h = 2 * c + e
                    mn = G[:, 23:25, :].rearrange("p o n -> p (o n)")[:, 0:3 * P]
                    sv = G[:, 25:27, :].rearrange("p o n -> p (o n)")[:, 0:3 * P]
                    pt = G[:, 27:29, :].rearrange("p o n -> p (o n)")[:, 0:3 * P]
                    dve.wait_ge(at_nc, h + 1)
                    link(nc.vector.tensor_tensor(mn, pm[:, 1, 0:3 * P], mask3, ALU.add))
                    dve.wait_ge(at_lg, h + 1)
                    nc.vector.scalar_tensor_tensor(out=sv[:, 0:P], in0=pm[:, 2, 0:P], scalar=stat[:, 44 + h:45 + h],
                                                   in1=mn[:, 0:P], op0=ALU.add, op1=ALU.add)
                    link(nc.vector.scalar_tensor_tensor(out=sv[:, P:3 * P], in0=pm[:, 2, P:3 * P],
                                                        scalar=stat[:, 52 + h:53 + h], in1=mn[:, P:3 * P],
                                                        op0=ALU.add, op1=ALU.add))
                    nc.vector.reduce_max(stat[:, 32:33], sv[:, 0:P], AX.X)
                    link(nc.vector.reduce_max(stat[:, 33:34], sv[:, P:3 * P], AX.X))
                    nc.vector.tensor_scalar(stat[:, 34:36], stat[:, 32:34], -1.0, None, ALU.mult).then_inc(at_max, 1)
                    dve.wait_ge(at_exp, h + 1)
                    link(nc.vector.reciprocal(stat[:, 38:40], stat[:, 36:38]))
                    nc.vector.tensor_scalar(sv[:, 0:P], sv[:, 0:P], stat[:, 38:39], None, ALU.mult)
                    nc.vector.tensor_scalar(sv[:, P:3 * P], sv[:, P:3 * P], stat[:, 39:40], None,
                                            ALU.mult).then_inc(at_p, 1)
                    dve.wait_ge(at_pt, h + 1)
                    nc.vector.tensor_copy(pt, pm[:, 2, 0:3 * P]).then_inc(at_ptc, 1)
                dve.wait_ge(y_high, 12 + c + 1)
                low(act_b[:, 12 + c:13 + c, :], G[:, 29:30, :], y_done)

            def merge_phases(gname, bname, buf, first):
                pend = skip_first(BY[gname + "0"])
                pend = phases([bname + "0", gname + "1", bname + "1", gname + "2", bname + "2", gname + "3"], pend)
                pieces(BY[bname + "3"], 0, 0)
                pend()
                for t in range(12):
                    dve.wait_ge(m_high, first + t + 1)
                    low(buf[:, t:t + 1, :], PJ[:, 16 + t:17 + t, :], m_low)
                return skip_first(BY[bname + "3"])

            pend = merge_phases("gates_a", "mix_a", act_a, 0)
            pend = phases(["w_out"], pend)
            pieces(BY["mlp_up0"], 0, 0)
            pend()
            pend = skip_first(BY["mlp_up0"], lambda: recip(1))
            pend = phases(["mlp_down0", "mlp_up1", "mlp_down1", "mlp_up2", "mlp_down2", "mlp_up3", "mlp_down3"], pend)
            pieces(BY["qkv2_0"], 0, 0)
            pend()
            pend = skip_first(BY["qkv2_0"], lambda: recip(2))
            for half in range(2):
                pieces(BY["qkv2_1" if half == 0 else "gates_b0"], 0, 0)
                pend()
                done = BY[f"qkv2_{half}"]
                dve.wait_ge(epi_done, done.unit0 + done.units + 2)
                if half == 0:
                    dve.wait_ge(in_c2, 16)
                for e in range(2):
                    h = 2 * half + e
                    if h:
                        dve.wait_ge(y_done, 16 + 4 * half + e)
                    for g in range(GROUPS):
                        last = nc.vector.tensor_scalar(PJ[:, 16 + g, :], G[:, 2 * g + e, :], HD2_SCALE, None, ALU.mult)
                    last.then_inc(b_q, 1)
                    dve.wait_ge(b_vps, h + 1)
                    nc.vector.tensor_copy(PJ[:, 25:27, :].rearrange("p o n -> p (o n)"), pm[:, 0, :])
                    nc.vector.tensor_copy(PJ[:, 27, :], pm[:, 1, 0:S]).then_inc(b_v, 1)
                    for q in range(2):
                        n = 2 * h + q
                        kw = P * (q + 1)
                        sv = PJ[:, 19:22, 0:kw]
                        dve.wait_ge(b_lg, n + 1)
                        for g in range(GROUPS):
                            last = nc.vector.scalar_tensor_tensor(
                                out=sv[:, g], in0=dist[:, g, 2 * P - kw:2 * P], scalar=slope(g * SLOTS + h),
                                in1=pm[:, g // 2, (g % 2) * S:(g % 2) * S + kw], op0=ALU.mult, op1=ALU.add)
                        link(last)
                        link(nc.vector.tensor_reduce(stat[:, 40:41], sv, AX.XY, ALU.max))
                        nc.vector.tensor_scalar(stat[:, 41:42], stat[:, 40:41], -1.0, None, ALU.mult).then_inc(b_max, 1)
                        dve.wait_ge(b_exp, n + 1)
                        link(nc.vector.reciprocal(stat[:, 43:44], stat[:, 42:43]))
                        nc.vector.tensor_scalar(sv, sv, stat[:, 43:44], None, ALU.mult).then_inc(b_p, 1)
                        dve.wait_ge(b_pt, n + 1)
                        nc.vector.tensor_copy(PJ[:, 22:24, 0:kw],
                                              pm[:, 0, :].rearrange("p (g n) -> p g n", g=2)[:, :, 0:kw])
                        nc.vector.tensor_copy(PJ[:, 24, 0:kw], pm[:, 1, 0:kw]).then_inc(b_ptc, 1)
                    dve.wait_ge(y_high, 16 + 4 * half + e + 1)
                    low(act_a[:, h:h + 1, :], PJ[:, 30:31, :], y_done)
                for e in range(2):
                    h = 2 * half + e
                    dve.wait_ge(y_done, 16 + 4 * half + 2 + e)
                    dve.wait_ge(s_z, 2 * h + 1)
                    nc.vector.tensor_copy(PJ[:, 17, :], pm[:, 2, 0:S])
                    nc.vector.tensor_scalar(PJ[:, 16, :], G[:, 18 + e, :], HD2_SCALE, None, ALU.mult).then_inc(s_abs, 1)
                    dve.wait_ge(s_z, 2 * h + 2)
                    nc.vector.tensor_copy(zview(PJ, 20), pm[:, 0, 0:3 * P]).then_inc(s_abs, 1)
                    dve.wait_ge(s_abs, 2 * h + 2)
                    dve.wait_ge(s_lnb, h + 1)
                    z3, l3, w3 = zview(PJ, 20), zview(PJ, 18), zview(PJ, 22)
                    link(nc.vector.scalar_tensor_tensor(out=l3, in0=z3, scalar=0.0, in1=l3, op0=ALU.max, op1=ALU.add))
                    nc.vector.scalar_tensor_tensor(out=l3[:, 0:S], in0=l3[:, 0:S], scalar=-1.0, in1=before01,
                                                   op0=ALU.mult, op1=ALU.mult)
                    nc.vector.scalar_tensor_tensor(out=l3[:, S:3 * P], in0=l3[:, S:3 * P], scalar=-1.0,
                                                   in1=before01[:, 0:P], op0=ALU.mult, op1=ALU.mult).then_inc(s_ln, 1)
                    dve.wait_ge(s_ln, h + 1)
                    link(nc.vector.tensor_tensor(z3, z3, l3, ALU.add))
                    nc.vector.tensor_tensor(z3[:, 0:S], z3[:, 0:S], before_neg, ALU.add)
                    link(nc.vector.tensor_tensor(z3[:, S:3 * P], z3[:, S:3 * P], before_neg[:, 0:P], ALU.add))
                    dve.wait_ge(s_suf, h + 1)
                    nc.vector.tensor_tensor(w3, z3, pm[:, 1, 0:3 * P], ALU.add).then_inc(s_logw, 1)
                    dve.wait_ge(y_high, 16 + 4 * half + 2 + e + 1)
                    low(act_a[:, 4 + h:5 + h, :], PJ[:, 30:31, :], y_done)
                if half == 0:
                    pend = skip_first(BY["qkv2_1"])
            pend = merge_phases("gates_b", "mix_b", act_b, 12)
            pend = phases(["w_out2"], pend)
            pieces(BY["ple"], 0, 0)
            pend()
            dve.wait_ge(p_high, 1)
            low(act_b[:, 0:2, :], PJ[:, 32:34, :], p_low)
            pend = skip_first(BY["ple"])
            pieces(BY["ffn_up0"], 0, 0)
            pend()

            def post_norm(n, first, post, gain):
                recip(n)
                for b in range(9):
                    if b < 8:
                        if b >= 2:
                            dve.wait_ge(pn_r, first // 2 + b - 1)
                        for t in range(2):
                            k = 2 * b + t
                            last = nc.vector.scalar_tensor_tensor(out=summ[:, b % 2, t], in0=PJ[:, 16 + k, :],
                                                                  scalar=pcol(post, k), in1=rstd[:],
                                                                  op0=ALU.mult, op1=ALU.mult)
                        last.then_inc(pn_t, 1)
                    if b:
                        for t in range(2):
                            k = 2 * (b - 1) + t
                            dve.wait_ge(pn_high, first + k + 1)
                            if gain:
                                nc.vector.scalar_tensor_tensor(
                                    out=act_a[:, k, S:2 * S], in0=PJ[:, k, :], scalar=pcol(gain, k),
                                    in1=act_a[:, k, 0:S].bitcast(F32), op0=ALU.mult,
                                    op1=ALU.subtract).then_inc(pn_low, 1)
                            else:
                                nc.vector.tensor_tensor(act_a[:, k, S:2 * S], PJ[:, k, :],
                                                        act_a[:, k, 0:S].bitcast(F32),
                                                        ALU.subtract).then_inc(pn_low, 1)
            dve.wait_ge(epi_done, BY["ffn_up0"].unit0 + 2)
            post_norm(3, 0, "g_mix_post2", "g_ffn_pre2")
            dve.wait_ge(pn_r, 8)
            pend = skip_first(BY["ffn_up0"], lambda: recip(4))
            pend = phases(["ffn_down0", "ffn_up1", "ffn_down1", "ffn_up2", "ffn_down2"], pend)
            pieces(BY["ple_gate"], 0, 0)
            pend()
            dve.wait_ge(epi_done, BY["ple_gate"].unit0 + 2)
            post_norm(5, 16, "g_ffn_post2", None)
            dve.wait_ge(pn_r, 16)
            pend = skip_first(BY["ple_gate"])
            pend()

        @block.gpsimd
        def _(pool):
            def link(ins):
                chain["pool"] += 1
                ins.then_inc(pool_chain, 1)
                pool.wait_ge(pool_chain, chain["pool"])

            def add_square(g, wait, value, inc):
                pool.wait_ge(wait, value)
                nc.gpsimd.tensor_tensor(sqacc[:], sqacc[:], sqt[:, g], ALU.add).then_inc(inc, 1)

            def apart():
                pool.sem_inc(pool_gate, 1)

            def epilogue(ph, i, j):
                k, g, n = ph.kind, j % 2, unit_no(ph, i, j)
                t0 = dst_tile(ph, i, j)
                s2 = summ[:, g]
                if k.startswith("branch"):
                    nb = 4 if k.startswith("branch4") else 2
                    if j % nb:
                        pool.wait_ge(scaled, after("scaled", ph, i, j))
                        pool.wait_ge(epi_done, n + 2)
                        d = tiles(PJ, t0 + 16, 2)
                        split = j % nb == nb - 1 and k.endswith("s")
                        apart()
                        nc.gpsimd.tensor_tensor(d, d, s2, ALU.add).then_inc(merged if split else epi_done, 1)
                elif k == "resid":
                    pool.wait_ge(summed, n + 1 + 2)
                    d = tiles(PJ, t0, 2)
                    apart()
                    nc.gpsimd.tensor_tensor(d, d, s2, ALU.add).then_inc(merged, 1)
                    v = after("squared", ph, i, j)
                    pool.wait_ge(sq_added, v + 1)
                    add_square(g, squared, v, sq_added)
                elif k == "accum":
                    pool.wait_ge(summed, n + 1 + 2)
                    d = tiles(PJ, t0 + (16 if ph.name.startswith("ffn") else 0), 2)
                    pool.wait_ge(epi_done, n + 2)
                    apart()
                    nc.gpsimd.tensor_tensor(d, d, s2, ALU.add).then_inc(epi_done, 1)
                elif k == "accsq":
                    pool.wait_ge(summed, n + 1 + 2)
                    d = tiles(PJ, t0 + 16, 2)
                    apart()
                    nc.gpsimd.tensor_tensor(d, d, s2, ALU.add).then_inc(merged, 1)
                    pool.wait_ge(merged, after("merged", ph, i, j))
                    pool.wait_ge(epi_done, n + 2)
                    pool.sem_inc(epi_done, 1)
                    v = after("squared", ph, i, j)
                    pool.wait_ge(sq_added, v + 1)
                    add_square(g, squared, v, sq_added)
                elif k == "mix":
                    v = after("squared", ph, i, j)
                    pool.wait_ge(sq_added, v + 1)
                    add_square(g, squared, v, sq_added)
                elif k == "final":
                    pool.wait_ge(scaled, after("scaled", ph, i, j))
                    d = tiles(PJ, t0, 2)
                    pool.wait_ge(epi_done, n + 2)
                    apart()
                    nc.gpsimd.tensor_tensor(d, d, s2, ALU.add).then_inc(epi_done, 1)

            def run(name):
                ph = BY[name]

                def body(i):
                    for j in range(ph.U):
                        epilogue(ph, i, j)
                over(pool, body, 0, ph.bodies)

            def reset(n):
                if n:
                    pool.wait_ge(ssq_ready, n)
                nc.gpsimd.memset(sqacc[:], 0.0).then_inc(acc_reset, 1)
                pool.wait_ge(acc_reset, n + 1)

            pool.sem_inc(sq_added, 2)
            reset(0)
            nc.gpsimd.memset(cbuf[:, 0:1024], 0.0).then_inc(bd_zeroed, 1)
            pool.wait_ge(bd_zeroed, 1)
            pool.dma_start(w_f, rows(A["w_in"])[:, :, N_F:N_F + HEADS]).then_inc(in_wf, 16)
            pool.dma_start(cbuf[:, 1664:2192], A["first"]).then_inc(in_c1, 16)
            for c in range(BT):
                pool.dma_start(pool_w[:, c, :], A["pool_w"][c]).then_inc(in_c1, 16)
                for e in range(2):
                    hs = slice(HD * e, HD * e + HD)
                    pool.dma_start(wr_bd[hs, c, hs], A["lru_wr"][2 * c + e]).then_inc(in_c1, 16)
                    pool.dma_start(wi_bd[hs, c, hs], A["lru_wi"][2 * c + e]).then_inc(in_c1, 16)
            for b in range(8):
                if b:
                    pool.wait_ge(sq0_added, b)
                add_square(b % 2, sq0_ready, b + 1, sq0_added)
            pool.wait_ge(lo0, 8)
            pool.dma_start(G[0:HEADS, 8:12, :], A["sel"].rearrange("p (a n) -> p a n", a=4)).then_inc(in_c1, 16)
            pool.wait_ge(epi_done, BY["gates_a0"].unit0 + 2)
            for c in range(BT):
                if c:
                    pool.wait_ge(pooled, c)
                src = PJ[:, 4 + c, :]
                for m in range(c + 1):
                    sh = 1 << m
                    dst = tile(G, 23 + m % 2)
                    nc.gpsimd.tensor_copy(dst[:, 0:sh], src[:, 0:sh])
                    link(nc.gpsimd.tensor_tensor(dst[:, sh:S], src[:, sh:S], src[:, 0:S - sh], ALU.add))
                    src = dst
                pool.sem_inc(win_ready, 1)
            pool.wait_ge(y_done, 16)
            pool.dma_start(resid, x_v).then_inc(in_resid, 16)
            pool.dma_start(cbuf[:, 0:1408], A["second"]).then_inc(in_c2, 16)
            for q in range(4):
                run(f"mix_a{q}")
            reset(1)
            pool.wait_ge(in_resid, 16)
            run("w_out")
            reset(2)
            for g in range(4):
                run(f"mlp_down{g}")
            for q in range(4):
                run(f"mix_b{q}")
            reset(3)
            run("w_out2")
            pool.dma_start(PJ[:, 32:34, :], p_v).then_inc(in_p, 16)

            def post_norm(n, first, squares):
                if squares:
                    reset(n + 1)
                for b in range(9):
                    if b < 8:
                        pool.wait_ge(pn_t, first // 2 + b + 1)
                        d = PJ[:, 2 * b:2 * b + 2, :]
                        nc.gpsimd.tensor_tensor(d, d, summ[:, b % 2], ALU.add).then_inc(pn_r, 1)
                    if b and squares:
                        if b > 1:
                            pool.wait_ge(pn_added, b - 1)
                        add_square((b - 1) % 2, pn_sq, b, pn_added)
            post_norm(3, 0, True)
            reset(5)
            run("ffn_down1")
            run("ffn_down2")
            post_norm(5, 16, False)
            run("ple_gate")


def kernel(**inputs):
    import concourse.bacc as _bacc
    from concourse.bass_utils import run_bass_kernel_spmd as _run

    a = {k: np.asarray(v) for k, v in inputs.items()}
    cols, npar = param_columns()

    def columns(v):
        v = v.reshape(-1, v.shape[-1] // P, P)
        return v.transpose(2, 0, 1).reshape(P, -1)

    fb = np.zeros((P, 1), np.float32)
    fb[0:HEADS, 0] = a["forget_b"][0]
    params = np.concatenate(
        [columns(a[k]) for k in ("norm_mix_g", "norm_mlp_g", "g_mix_pre_2", "g_mix_post_2", "g_ffn_pre_2",
                                 "g_ffn_post_2")]
        + [columns(a["lru_conv_w"][0]), columns(a["lru_conv_b"]), columns(a["lru_br"]), columns(a["lru_bi"]),
           columns(a["lru_lambda"]), columns(a["pool_scale"]), columns(a["sconv_w"][0]),
           np.concatenate([a["q_norm_g"], a["q_norm_g"]], 1).T, np.concatenate([a["k_norm_g"], a["k_norm_g"]], 1).T,
           fb, columns(a["conv_w_2"][0]), columns(a["conv_b_2"])], 1)
    common, first, sel, second = constants()
    arrays = {
        "x_t": a["x"][0].T, "p_t": a["p_2"][0, 0].T, "params": params, "common": common, "first": first,
        "sel": sel, "second": second, "w_in": a["w_in"][0], "w_branch": a["w_branch"][0].reshape(D, D),
        "lru_wr": a["lru_wr"][0], "lru_wi": a["lru_wi"][0], "pool_w": a["pool_w"][0],
    }
    for k in ("w_out", "w_mlp_up", "w_mlp_down", "w_in_2", "w_branch_a_2", "w_branch_b_2", "w_out_2", "w_up_2",
              "w_down_2", "w_ple_in_2", "w_ple_gate_2"):
        arrays[k] = a[k][0]
    arrays = {k: np.ascontiguousarray(v) for k, v in arrays.items()}

    nc = _bacc.Bacc("TRN2", target_bir_lowering=False, num_devices=1)
    A = {k: nc.dram_tensor("in_" + k, v.shape, F32, kind="ExternalInput").ap() for k, v in arrays.items()}
    out = nc.dram_tensor("out_t", (D, S), F32, kind="ExternalOutput").ap()
    build(nc, A, out)
    r = _run(nc, [{"in_" + k: v for k, v in arrays.items()}], core_ids=[0])
    return np.ascontiguousarray(np.asarray(r.results[0]["out_t"]).T)[None]
```

```python
from contextlib import ExitStack

import numpy as np
import concourse.bass as bass
from concourse import mybir

F32 = mybir.dt.float32
F32R = mybir.dt.float32r
ACT = mybir.ActivationFunctionType
ALU = mybir.AluOpType
AX = mybir.AxisListType

P = 128
S = 256
D = 2048
KT = D // P
BW = 512
BT = BW // P
DFF = 8192
DFF2 = 5632
N_F = 4096
N_G = 4104
HEADS = 8
HD = 64
N_G2 = 6144
SLOTS = 4
GROUPS = 3
EPS = 1e-6
NEG = -1.0e30
RING = 4
TINY = 2.0 ** -116
HD2_SCALE = 128.0 ** -0.5


def param_columns():
    sizes = [("g_mix", 16), ("g_mlp", 16), ("g_mix_pre2", 16), ("g_mix_post2", 16), ("g_ffn_pre2", 16),
             ("g_ffn_post2", 16), ("lru_conv_w", 16), ("lru_conv_b", 4), ("lru_br", 4), ("lru_bi", 4),
             ("lru_lambda", 4), ("pool_scale", 4), ("sconv_w", 12), ("q_g", 1), ("k_g", 1), ("forget_b", 1),
             ("conv_w2", 3 * 88), ("conv_b2", 88)]
    at, cols = 0, {}
    for name, n in sizes:
        cols[name] = at
        at += n
    return cols, at


def slope(head):
    return float(np.float32(2.0) ** np.float32(-8.0 * (head + 1) / (SLOTS * GROUPS)))


def constants():
    p = np.arange(P)[:, None]
    f = np.arange(P)[None, :]
    ident = (p == f)
    ones = np.ones((P, P))
    common = np.concatenate([ident, ones], 1).astype(np.float32)
    same_head = (p // HD == f // HD)
    causal = np.where(f <= p, 0.0, NEG)
    mask3 = np.concatenate([causal, np.zeros((P, P)), causal], 1)
    inv = np.broadcast_to(1.0 / (np.arange(16) + 1.0), (P, 16))
    first = np.concatenate([same_head, mask3, inv], 1).astype(np.float32)
    sel = np.zeros((HEADS, HEADS, P), np.float32)
    for h in range(HEADS):
        sel[h, h] = 1.0
    dist = (P + p) - np.arange(2 * P)[None, :]
    groups = []
    for span, dil in ((128, 1), (512, 4), (2048, 16)):
        ok = (dist >= 0) & (dist % dil == 0) & (dist <= span)
        groups.append(np.where(ok, -dist, NEG))
    strict = p < f
    before01 = np.concatenate([strict, np.ones((P, P))], 1)
    before_neg = np.where(before01 > 0, 0.0, NEG)
    later = (p > f)
    second = np.concatenate(groups + [before01, before_neg, later], 1).astype(np.float32)
    return common, first, sel.reshape(HEADS, HEADS * P), second


class Phase:

    def __init__(self, kind, units, U, ppu, name, quarter=0, group=0, half=0):
        self.kind, self.units, self.U, self.ppu, self.name = kind, units, U, ppu, name
        self.quarter, self.group, self.half = quarter, group, half
        self.piece0 = self.unit0 = self.bodies = 0
        self.count0 = {}


ADDS = {
    "scaled": {"gate": [1, 1, 1, 1], "branch4": [0, 1, 1, 1], "branch4s": [0, 1, 1, 1], "branch2": [0, 1, 0, 1],
               "branch2s": [0, 1, 0, 1], "up": [1, 1], "upconv": [1, 1], "final": [1, 1]},
    "acted": {"up": [1, 1], "upconv": [1, 1], "final": [1, 1]},
    "conv_base": {"upconv": [1, 1]},
    "conv_tap": {"upconv": [2, 2]},
    "conv_done": {"upconv": [0, 1]},
    "merged": {"branch4s": [0, 0, 0, 1], "branch2s": [0, 1, 0, 1], "resid": [1, 1], "accsq": [1, 1, 1, 1]},
    "high_out": {"branch4s": [0, 0, 0, 1], "branch2s": [0, 1, 0, 1], "up": [1, 1], "resid": [1, 1],
                 "upconv": [0, 1]},
    "squared": {"resid": [1, 1], "mix": [1, 1], "accsq": [1, 1, 1, 1]},
    "sq_added": {"resid": [1, 1], "mix": [1, 1], "accsq": [1, 1, 1, 1]},
}


def plan():
    ph = [Phase("proj", 10, 2, 4, name="proj_a"), Phase("proj", 6, 2, 4, name="proj_b")]
    for step, q in (("gates", 0), ("gates", 1), ("mix", 0), ("mix", 1),
                    ("gates", 2), ("mix", 2), ("gates", 3), ("mix", 3)):
        if step == "gates":
            ph.append(Phase("gate", 8, 2, 4, name=f"gates_a{q}", quarter=q))
        else:
            ph.append(Phase("branch4s" if q == 3 else "branch4", 8, 4, 1, name=f"mix_a{q}", quarter=q))
    ph.append(Phase("resid", 8, 2, 4, name="w_out"))
    for g in range(4):
        ph.append(Phase("up", 8, 2, 4, name=f"mlp_up{g}", group=g))
        ph.append(Phase("resid" if g == 3 else "accum", 8, 2, 4, name=f"mlp_down{g}", group=g))
    for h in range(2):
        ph.append(Phase("proj", 8, 2, 4, name=f"slots{h}", half=h))
        ph.append(Phase("proj", 1, 1, 4, name=f"slots{h}_end", half=h))
    ph.append(Phase("proj", 6, 2, 4, name="stick"))
    for h in range(2):
        ph.append(Phase("gate", 8, 4, 4, name=f"gates_b{h}", half=h))
        ph.append(Phase("branch2s" if h else "branch2", 8, 4, 1, name=f"mix_b{h}", half=h))
    ph.append(Phase("mix", 8, 2, 4, name="w_out2"))
    ph.append(Phase("store", 8, 4, 1, name="ple"))
    for g, n in enumerate((8, 8, 6)):
        ph.append(Phase("upconv", 2 * n, 2, 4, name=f"ffn_up{g}", group=g))
        if g == 2:
            ph.append(Phase("accsq", 8, 4, 3, name="ffn_down2", group=g))
        else:
            ph.append(Phase("store" if g == 0 else "accum", 8, 2, 4, name=f"ffn_down{g}", group=g))
    ph.append(Phase("final", 8, 2, 4, name="ple_gate"))
    piece = unit = 0
    count = {k: 0 for k in ADDS}
    for x in ph:
        assert x.units % x.U == 0 and (x.U % 2 == 0 or x.units == 1) and (x.U * x.ppu) % RING == 0
        x.piece0, x.unit0, x.bodies = piece, unit, x.units // x.U
        x.count0 = dict(count)
        piece += x.units * x.ppu
        unit += x.units
        for k, kinds in ADDS.items():
            count[k] += x.bodies * sum(kinds.get(x.kind, [0])[:x.U])
    return ph


def unit_no(ph, i, j):
    return i * ph.U + (ph.unit0 + j)


def piece_no(ph, i, j, s):
    return i * (ph.U * ph.ppu) + (ph.piece0 + j * ph.ppu + s)


def after(name, ph, i, j):
    adds = ADDS[name][ph.kind][:ph.U]
    return i * sum(adds) + (ph.count0[name] + sum(adds[:j + 1]))


def tiles(buf, at, n=1):
    if isinstance(at, int):
        return buf[:, at:at + n, :]
    return buf[:, bass.ds(at, n), :]


def tile(buf, at):
    return tiles(buf, at).rearrange("p o n -> p (o n)")


def flat3(buf, t):
    return buf[:, t:t + 3, :].rearrange("p o n -> p (o n)").rearrange("p (e n) -> p e n", e=2)


def zview(buf, t):
    return buf[:, t:t + 2, :].rearrange("p o n -> p (o n)")[:, 0:3 * P]


def build(nc, A, out):
    PH = plan()
    BY = {x.name: x for x in PH}
    COL, NPAR = param_columns()

    with ExitStack() as ctx:
        def sb(name, shape, dt=F32):
            return ctx.enter_context(nc.sbuf_tensor(name, shape, dt))

        def sem(name):
            return ctx.enter_context(nc.semaphore(name))

        raw = sb("raw", [P, RING, 4 * S])
        wh = sb("w_high", [P, RING, 4 * S], F32R)
        wl = sb("w_low", [P, RING, 4 * S], F32R)
        act_a = sb("act_a", [P, KT, 2 * S], F32R)
        act_b = sb("act_b", [P, KT, 2 * S], F32R)
        G = sb("gates", [P, 32, S])
        PJ = sb("proj", [P, 34, S])
        par = sb("params", [P, NPAR])
        common = sb("common", [P, 2 * P])
        cbuf = sb("small_ops", [P, 2192])
        bcopy = sb("bcopy", [P, 2, 2, S])
        summ = sb("summ", [P, 2, 2, S])
        sqt = sb("sqt", [P, 2, 2, S])
        sqacc = sb("sqacc", [P, 2, S])
        rstd = sb("rstd", [P, S])
        rms_buf = sb("rms", [P, S])
        stat = sb("stat", [P, 66])
        ps = ctx.enter_context(nc.psum_tensor("ps_gemm", [P, 2, 2, 2 * S], F32))
        pm = ctx.enter_context(nc.psum_tensor("ps_small", [P, 4, 2 * S], F32))

        ident, ones = common[:, 0:P], common[:, P:2 * P]
        wr_bd = cbuf[:, 0:512].rearrange("p (c n) -> p c n", c=4)
        wi_bd = cbuf[:, 512:1024].rearrange("p (c n) -> p c n", c=4)
        pool_w = cbuf[:, 1024:1536].rearrange("p (c n) -> p c n", c=4)
        w_f = cbuf[:, 1536:1664].rearrange("p (k n) -> p k n", k=KT)
        same_head = cbuf[:, 1664:1792]
        mask3 = cbuf[:, 1792:2176]
        inv16 = cbuf[:, 2176:2192]
        dist = cbuf[:, 0:768].rearrange("p (g n) -> p g n", g=GROUPS)
        before01 = cbuf[:, 768:1024]
        before_neg = cbuf[:, 1024:1280]
        later = cbuf[:, 1280:1408]
        sel_t = cbuf[0:HEADS, 0:1024].rearrange("p (h n) -> p h n", h=HEADS)
        onesrow = G[:, 12, :]

        resid = PJ[:, 0:KT, :]
        merged_m = PJ[:, KT:2 * KT, :]

        def pcol(name, i=0):
            c = COL[name]
            if isinstance(i, int):
                return par[:, c + i:c + i + 1]
            return par[:, bass.ds(i + c, 1)]

        MERGE_A = ["mix_a0", "mix_a1", "gates_a2", "mix_a2", "gates_a3"]
        MERGE_B = ["mix_b0", "gates_b1"]

        raw_full = [sem(f"raw_full{s}") for s in range(RING)]
        high_ready = sem("high_ready")
        split_done = sem("split_done")
        w_used = sem("w_used")
        b_copied = sem("b_copied")
        summed = sem("summed")
        epi_done = sem("epi_done")
        step = {k: sem(k) for k in ADDS}
        scaled, acted, conv_base = step["scaled"], step["acted"], step["conv_base"]
        conv_tap, conv_done = step["conv_tap"], step["conv_done"]
        merged, high_out, squared, sq_added = step["merged"], step["high_out"], step["squared"], step["sq_added"]

        in_par, in_common, in_c1, in_wf, in_sel, in_c2, in_p, in_resid = (
            sem("in_" + n) for n in ("params", "common", "consts1", "w_f", "selectors", "consts2", "p", "resid"))
        in_x = [sem(f"in_x{b}") for b in range(4)]
        stored = sem("stored")
        sq0_ready, sq0_added, hi0, lo0 = sem("sq0_ready"), sem("sq0_added"), sem("hi0"), sem("lo0")
        acc_reset, ssq_ready, rms_ready, rstd_ready = (
            sem("acc_reset"), sem("ssq_ready"), sem("rms_ready"), sem("rstd_ready"))
        act_chain, dve_chain, pool_chain = sem("act_chain"), sem("dve_chain"), sem("pool_chain")
        chain = {"act": 0, "dve": 0, "pool": 0}
        act_gate, pool_gate = sem("act_gate"), sem("pool_gate")
        zeroed, bd_zeroed = sem("zeroed"), sem("bd_zeroed")
        y_high, y_done = sem("y_high"), sem("y_done")
        f_logits, f_biased, f_log, cum_ready, cumt_ps, cumt_ready = (
            sem(n) for n in ("f_logits", "f_biased", "f_log", "cum_ready", "cumt_ps", "cumt_ready"))
        nscale_ready, sp_exp = sem("nscale_ready"), sem("sp_exp")
        lru_base, lru_u, lru_ps, lru_act, lru_pre, lru_sqrt, lru_h = (
            sem(n) for n in ("lru_base", "lru_u", "lru_ps", "lru_act", "lru_pre", "lru_sqrt", "lru_h"))
        win_ready, pooled, pool_ps, pool_y = (sem(n) for n in ("win_ready", "pooled", "pool_ps", "pool_y"))
        sc_z, sc_base, sc_y = sem("sc_z"), sem("sc_base"), sem("sc_y")
        at_sq, at_ssq, at_rms, at_qk, at_vps, at_v = (
            sem(n) for n in ("at_sq", "at_ssq", "at_rms", "at_qk", "at_vps", "at_v"))
        at_lg, at_max, at_exp, at_ri, at_p, at_pt, at_ptc, at_o = (
            sem(n) for n in ("at_lg", "at_max", "at_exp", "at_ri", "at_p", "at_pt", "at_ptc", "at_o"))
        b_q, b_vps, b_v, b_lg, b_max, b_exp, b_ri, b_p, b_pt, b_ptc, b_o = (
            sem("b_" + n) for n in ("q", "vps", "v", "lg", "max", "exp", "ri", "p", "pt", "ptc", "o"))
        s_z, s_abs, s_ln, s_lnb, s_suf, s_logw, s_w, s_o = (
            sem("s_" + n) for n in ("z", "abs", "ln", "lnb", "suf", "logw", "w", "o"))
        m_high, m_low = sem("m_high"), sem("m_low")
        p_high, p_low = sem("p_high"), sem("p_low")
        pn_t, pn_r, pn_high, pn_low, pn_sq, pn_added = (
            sem("pn_" + n) for n in ("t", "r", "high", "low", "sq", "added"))

        def rows(w):
            return w.rearrange("(t p) n -> p t n", p=P)

        W = {k: rows(A[k]) for k in ("w_in", "w_branch", "w_out", "w_mlp_up", "w_mlp_down", "w_in_2",
                                     "w_branch_a_2", "w_branch_b_2", "w_out_2", "w_up_2", "w_down_2",
                                     "w_ple_in_2", "w_ple_gate_2")}
        x_v = rows(A["x_t"])
        p_v = rows(A["p_t"])
        out_v = rows(out)

        def source(ph, i, j, s):
            u = i * ph.U + j
            n, q = ph.name, ph.quarter
            k0, kn = 4 * s, 4
            if n == "proj_a":
                w, c = "w_in", u * 256
            elif n == "proj_b":
                w, c = "w_in", u * 256 + 2560
            elif n.startswith("slots"):
                w, c = "w_in_2", (u + (8 if n.endswith("end") else 0)) * 512 + ph.half * 256
            elif n == "stick":
                w, c = "w_in_2", u * 256 + 36 * P
            elif n.startswith("gates_b"):
                w, c = "w_in_2", i * D + (N_G2 + ph.half * 1024 + j * 256)
            elif n.startswith("gates_a"):
                w, c = "w_in", i * D + (N_G + q * 512 + j * 256)
            elif n.startswith("mix_b"):
                w, c = ("w_branch_a_2", "w_branch_b_2")[j % 2], i * 512 + (ph.half * 1024 + j // 2 * 256)
            elif n.startswith("mix_a"):
                w, c, k0 = "w_branch", i * 256 + q * 512, 4 * j
            elif n == "w_out":
                w, c = "w_out", u * 256
            elif n == "w_out2":
                w, c = "w_out_2", u * 256
            elif n.startswith("ffn_up"):
                w, c = "w_up_2", i * 256 + (j * DFF2 + ph.group * D)
            elif n.startswith("mlp_up"):
                w, c = "w_mlp_up", u * 256 + ph.group * D
            elif n.startswith("ffn_down"):
                w, c, k0 = "w_down_2", u * 256, 16 * ph.group + 4 * s
            elif n.startswith("mlp_down"):
                w, c, k0 = "w_mlp_down", u * 256, 16 * ph.group + 4 * s
            elif n == "ple":
                w, c, kn = "w_ple_in_2", u * 256, 2
            else:
                w, c = "w_ple_gate_2", u * 256
            cols = slice(c, c + 256) if isinstance(c, int) else bass.ds(c, 256)
            return W[w][:, k0:k0 + kn, cols]

        def slot(ph, j, s):
            return (j * ph.ppu + s) % RING

        def over(eng, body, start, end):
            if end - start > 1:
                with eng.Fori(start, end) as i:
                    body(i)
            elif end > start:
                body(start)

        def skewed(eng, pending, ph, pieces, epilogue, started=False, once=None):
            U, last = ph.U, ph.bodies - 1
            if not started:
                pieces(ph, 0, 0)
            if pending:
                pending()

            def body(i):
                for j in range(U):
                    if j + 1 < U:
                        pieces(ph, i, j + 1)
                    else:
                        pieces(ph, i + 1, 0)
                    if once and isinstance(i, int) and i == 0 and j == 0:
                        once()
                    epilogue(ph, i, j)
            if once:
                assert last > 0
                body(0)
            over(eng, body, 1 if once else 0, last)
            for j in range(U - 1):
                pieces(ph, last, j + 1)
                epilogue(ph, last, j)
            return lambda: epilogue(ph, last, U - 1)

        def threaded(eng, pending, ph, piece, stages, started=False, once=None):
            U, last = ph.U, ph.bodies - 1

            def pieces(i, j):
                for s in range(ph.ppu):
                    piece(ph, i, j, s)
            if not started:
                pieces(0, 0)
                if ph.ppu == 1:
                    pieces(0, 1)
            if pending:
                pending()
            if started or ph.ppu > 1:
                pieces(0, 1)
            if once:
                once()

            def body(i, end=False):
                for j in range(U - 1 if end else U):
                    steps = stages(ph, i, j)
                    for s in range(max(len(steps), ph.ppu)):
                        if s < len(steps):
                            steps[s]()
                        if s < ph.ppu and (j + 2 < U or not end):
                            if j + 2 < U:
                                piece(ph, i, j + 2, s)
                            else:
                                piece(ph, i + 1, j + 2 - U, s)
            over(eng, body, 0, last)
            body(last, True)

            def finish():
                for step in stages(ph, last, U - 1):
                    step()
            return finish

        def fed(pending, phases, piece, epilogue, ended):
            for ph in phases:
                for i in range(ph.bodies):
                    for j in range(ph.U):
                        for s in range(ph.ppu):
                            piece(ph, i, j, s)
                            if s == ph.ppu - 1:
                                if pending:
                                    pending()
                                pending = (lambda ph=ph, i=i, j=j: epilogue(ph, i, j))
                            yield
            ended.append(pending)

        def take(stream, n=None):
            for _ in stream if n is None else range(n):
                if n is not None:
                    next(stream, None)

        def bank(ph, j):
            return (ph.unit0 + j) % 2

        def end_piece(ph, i, j):
            return piece_no(ph, i, j, ph.ppu - 1) + 1 + RING

        def dst_tile(ph, i, j):
            q, n, u = ph.quarter, ph.name, i * ph.U + j
            if n == "proj_b":
                return u * 2 + 20
            if n.startswith("slots0"):
                return u * 2 + (16 if n.endswith("end") else 0)
            if n.startswith("slots1"):
                return u * 2 + (16 if n.endswith("end") else 0) + 18
            if n.startswith("gates_b"):
                return u * 2 + 12
            if ph.kind == "gate":
                return i * 4 + 2 * j
            if ph.kind.startswith("branch4"):
                return i * 2 + 4 * q
            if ph.kind.startswith("branch2"):
                return i * 4 + (8 * ph.half + 2 * (j // 2))
            if ph.kind == "upconv":
                return i * 2
            return u * 2

        def gate_tiles(ph, t):
            return tiles(PJ if ph.name in ("gates_a1", "mix_a1") else G, t, 2)

        def proj_tiles(ph, t0):
            if ph.name.startswith("proj"):
                return tiles(PJ, t0, 2)
            if isinstance(t0, int) and t0 >= 32:
                return tiles(PJ, t0 - 32 + 16, 2)
            return tiles(G, t0, 2)

        def slot_tile(half, k):
            t = 18 * half + k
            return G[:, t, :] if t < 32 else PJ[:, t - 32 + 16, :]

        def group_bank(q, g):
            if q == 0:
                return pm[:, 2, g * P:g * P + P]
            return pm[:, g // 2, (g % 2) * S:(g % 2) * S + S]

        def by_query(t, q):
            flat = PJ[:, t:t + 5, :].rearrange("p o n -> p (o n)")
            if q == 0:
                return flat[:, 0:3 * P].rearrange("p (g n) -> p g n", g=GROUPS)
            return flat[:, 3 * P:9 * P].rearrange("p (g n) -> p g n", g=GROUPS)

        def probs(q):
            return by_query(25, q)

        def probs_t(q):
            return by_query(20, q)

        block = ctx.enter_context(nc.Block())

        @block.sync
        def _(sp):
            sp.sem_inc(split_done, RING)
            for b in range(4):
                sp.dma_start(tiles(G, 4 * b, 4), x_v[:, 4 * b:4 * b + 4, :]).then_inc(in_x[b], 16)
            sp.dma_start(par[:], A["params"]).then_inc(in_par, 16)
            sp.dma_start(common[:], A["common"]).then_inc(in_common, 16)
            for ph in PH:
                def body(i, ph=ph):
                    for j in range(ph.U):
                        for s in range(ph.ppu):
                            n, at = piece_no(ph, i, j, s), slot(ph, j, s)
                            src = source(ph, i, j, s)
                            kn = src.shape[1]
                            sp.wait_ge(split_done, n + 1)
                            sp.dma_start(raw[:, at, 0:kn * S].rearrange("p (t n) -> p t n", t=kn),
                                         src).then_inc(raw_full[at], 16)
                over(sp, body, 0, ph.bodies)
            fin = BY["ple_gate"]
            for u in range(8):
                sp.wait_ge(epi_done, fin.unit0 + u + 1 + 2)
                sp.dma_start(out_v[:, 2 * u:2 * u + 2, :], tiles(PJ, 2 * u, 2)).then_inc(stored, 16)
            sp.wait_ge(stored, 8 * 16)

        @block.tensor
        def _(pe):
            pe.sem_inc(w_used, RING)

            def high(t):
                return t[:, 0:S]

            def piece(ph, x_in, need, i, j, s):
                n, g, at = unit_no(ph, i, j), bank(ph, j), slot(ph, j, s)
                kn = 2 if ph.name == "ple" else 4
                if s == 0:
                    pe.wait_ge(summed, n + 1)
                if need:
                    need(i, j, s)
                pe.wait_ge(split_done, piece_no(ph, i, j, s) + 1 + RING)
                for k in range(kn):
                    x = x_in(i, j, 4 * s + k)
                    first = s == 0 and k == 0
                    final = s == ph.ppu - 1 and k == kn - 1
                    for t in range(2):
                        o = k * S + t * P
                        nc.tensor.matmul(ps[:, g, t, :], wh[:, at, o:o + P], x,
                                         start=first, stop=False, skip_group_check=True)
                        last = nc.tensor.matmul(ps[:, g, t, 0:S], wl[:, at, o:o + P], high(x),
                                                start=False, stop=final, skip_group_check=True)
                last.then_inc(w_used, 1)

            def units(ph, x_in, need=None, once=None):
                def body(i):
                    for j in range(ph.U):
                        for s in range(ph.ppu):
                            piece(ph, x_in, need, i, j, s)
                        if once and isinstance(i, int) and i == 0 and j == 0:
                            once()
                if once:
                    body(0)
                over(pe, body, 1 if once else 0, ph.bodies)

            def straight(phases):
                for ph, x_in, need in phases:
                    for i in range(ph.bodies):
                        for j in range(ph.U):
                            for s in range(ph.ppu):
                                piece(ph, x_in, need, i, j, s)
                                yield

            def from_buf(buf):
                return lambda i, j, k: buf[:, k, :]

            def ssq(n, ready, value):
                pe.wait_ge(ready, value)
                if n:
                    pe.wait_ge(rms_ready, n)
                nc.tensor.matmul(pm[:, 3, 0:S], ones, sqacc[:, 0, :], start=True, stop=False)
                nc.tensor.matmul(pm[:, 3, 0:S], ones, sqacc[:, 1, :], start=False, stop=True).then_inc(ssq_ready, 1)

            pe.wait_ge(in_common, 16)
            def need_x(i, j, s):
                pe.wait_ge(lo0, 2 * (s + 1))
            units(BY["proj_a"], from_buf(act_a), need_x, lambda: ssq(0, sq0_added, 8))

            pe.wait_ge(in_wf, 16)
            for k in range(KT):
                for half in range(2):
                    last = nc.tensor.matmul(pm[0:HEADS, 0, 0:S], w_f[:, k, :],
                                            act_a[:, k, half * S:half * S + S].bitcast(F32),
                                            start=(k == 0 and half == 0), stop=(k == KT - 1 and half == 1))
            last.then_inc(f_logits, 1)

            fill = straight([(BY["proj_b"], from_buf(act_a), None), (BY["gates_a0"], from_buf(act_a), None),
                             (BY["gates_a1"], from_buf(act_a), None)])
            pe.wait_ge(in_c1, 21 * 16)
            for c in range(BT):
                take(fill, 3)
                pe.wait_ge(lru_u, 3 * (c + 1))
                if c:
                    pe.wait_ge(lru_act, c)
                nc.tensor.matmul(pm[:, 1, 0:S], wr_bd[:, c, :], tile(G, 16), start=True, stop=True)
                nc.tensor.matmul(pm[:, 1, S:2 * S], wi_bd[:, c, :], tile(G, 16), start=True,
                                 stop=True).then_inc(lru_ps, 1)
                pe.wait_ge(pooled, c + 1)
                if c:
                    pe.wait_ge(pool_y, c)
                nc.tensor.matmul(pm[:, 2, 0:S], pool_w[:, c, :], tile(G, 25), start=True,
                                 stop=True).then_inc(pool_ps, 1)
                if c == 0:
                    pe.wait_ge(cum_ready, 1)
                    for q in range(2):
                        last = nc.tensor.transpose(pm[:, 0, 256 + 8 * q:264 + 8 * q],
                                                   PJ[0:HEADS, 32, q * P:q * P + P], ident[0:HEADS, 0:HEADS])
                    last.then_inc(cumt_ps, 1)
                take(fill, 3)
            pe.wait_ge(cumt_ready, 1)
            for c in range(BT):
                take(fill, 2)
                pe.wait_ge(at_sq, c + 1)
                if c:
                    pe.wait_ge(y_high, 12 + c)
                nc.tensor.matmul(pm[:, 0, :], same_head, G[:, 16:18, :].rearrange("p o n -> p (o n)"),
                                 start=True, stop=True).then_inc(at_ssq, 1)
                if c:
                    pe.wait_ge(at_max, c)
                else:
                    pe.wait_ge(lru_act, BT)
                for q in range(2):
                    last = nc.tensor.transpose(pm[:, 1, q * P:q * P + P], PJ[:, 28 + c, q * P:q * P + P], ident)
                last.then_inc(at_vps, 1)
                take(fill, 6)
                pe.wait_ge(at_qk, c + 1)
                pe.wait_ge(at_v, c + 1)
                if c:
                    pe.wait_ge(at_ptc, c)
                else:
                    pe.wait_ge(in_sel, 16)
                    pe.wait_ge(pool_y, BT)
                    pe.wait_ge(rms_ready, 1)
                for e in range(2):
                    h = 2 * c + e
                    nc.tensor.matmul(pm[:, 1 - e, 0:P], sel_t[:, h, :], PJ[0:HEADS, 33, 0:P],
                                     start=True, stop=True)
                    nc.tensor.matmul(pm[:, 1 - e, P:3 * P], sel_t[:, h, :], PJ[0:HEADS, 33, :],
                                     start=True, stop=True)
                    qk = slice(HD * e, HD * e + HD)
                    nc.tensor.matmul(pm[:, 2 + e, 0:P], G[qk, 20, 0:P], G[qk, 21, 0:P], start=True, stop=True)
                    last = nc.tensor.matmul(pm[:, 2 + e, P:3 * P], G[qk, 20, P:S], G[qk, 21, :], start=True,
                                            stop=True)
                last.then_inc(at_lg, 1)
                take(fill, 5)
                pe.wait_ge(at_p, c + 1)
                for e in range(2):
                    for b in range(3):
                        last = nc.tensor.transpose(pm[:, 2 + e, b * P:b * P + P],
                                                   flat3(G, 26)[:, e, b * P:b * P + P], ident)
                last.then_inc(at_pt, 1)
                take(fill, 3)
                pe.wait_ge(at_ptc, c + 1)
                for e in range(2):
                    qk = slice(HD * e, HD * e + HD)
                    pt = flat3(G, 29)[:, e]
                    nc.tensor.matmul(pm[qk, 0, 0:P], G[:, 22, qk], pt[:, 0:P], start=True, stop=True)
                    nc.tensor.matmul(pm[qk, 0, P:S], G[:, 22, qk], pt[:, P:2 * P], start=True, stop=False)
                    last = nc.tensor.matmul(pm[qk, 0, P:S], G[:, 22, P + HD * e:P + HD * e + HD], pt[:, 2 * P:3 * P],
                                            start=False, stop=True)
                last.then_inc(at_o, 1)
            take(fill)

            for q in range(4):
                if q > 1:
                    units(BY[f"gates_a{q}"], from_buf(act_a))

                def need_y(i, j, s):
                    pe.wait_ge(y_done, 16)
                units(BY[f"mix_a{q}"], lambda i, j, k: act_b[:, 4 * j + k, :], need_y)

            def after_phase(name, extra=None):
                src = BY[name]

                def need(i, j, s):
                    done = (src.unit0 + min(src.units, 2 * (s + 1))) if src.kind != "upconv" else (
                        src.unit0 + min(src.units, 4 * (s + 1)))
                    if extra:
                        extra(s)
                    pe.wait_ge(epi_done, done + 2)
                return need

            def need_m(i, j, s):
                if s < 3:
                    pe.wait_ge(m_low, 4 * (s + 1))
                else:
                    pe.wait_ge(epi_done, BY["mix_a3"].unit0 + 8 + 2)
            units(BY["w_out"], from_buf(act_a), need_m)
            for g in range(4):
                if g == 0:
                    units(BY["mlp_up0"], from_buf(act_b), after_phase("w_out"),
                          lambda: ssq(1, sq_added, BY["w_out"].count0["sq_added"] + 8 + 2))
                else:
                    units(BY[f"mlp_up{g}"], from_buf(act_b))
                units(BY[f"mlp_down{g}"], from_buf(act_a), after_phase(f"mlp_up{g}"))

            units(BY["slots0"], from_buf(act_b), after_phase("mlp_down3"),
                  lambda: ssq(2, sq_added, BY["mlp_down3"].count0["sq_added"] + 8 + 2))
            units(BY["slots0_end"], from_buf(act_b))

            pe.wait_ge(in_c2, 16)
            for half in range(2):
                names, f = ((["slots1", "slots1_end"], (4, 3, 7, 4)), (["stick"], (3, 2, 4, 3)))[half]
                fill = straight([(BY[x], from_buf(act_b), None) for x in names])
                for e in range(2):
                    h = 2 * half + e
                    take(fill, f[0])
                    if h:
                        pe.wait_ge(y_high, 16 + h)
                    pe.wait_ge(epi_done, BY[f"slots{half}_end"].unit0 + 1 + 2)
                    for g in range(GROUPS):
                        for q in range(2):
                            last = nc.tensor.transpose(
                                pm[:, g // 2, (g % 2) * S + q * P:(g % 2) * S + q * P + P],
                                slot_tile(half, 12 + 2 * g + e)[:, q * P:q * P + P], ident)
                    last.then_inc(b_vps, 1)
                    take(fill, f[1])
                    pe.wait_ge(b_q, h + 1)
                    pe.wait_ge(b_v, h + 1)
                    for q in range(2):
                        for g in range(GROUPS):
                            last = nc.tensor.matmul(group_bank(q, g), PJ[:, 20 + g, q * P:q * P + P],
                                                    slot_tile(half, 6 + 2 * g + e)[:, 0:P * (q + 1)],
                                                    start=True, stop=True)
                    last.then_inc(b_lg, 1)
                    take(fill, f[2])
                    pe.wait_ge(b_p, h + 1)
                    for q in range(2):
                        for g in range(GROUPS):
                            for kt in range(q + 1):
                                last = nc.tensor.transpose(group_bank(q, g)[:, kt * P:kt * P + P],
                                                           probs(q)[:, g, kt * P:kt * P + P], ident)
                    last.then_inc(b_pt, 1)
                    take(fill, f[3])
                    pe.wait_ge(b_ptc, h + 1)
                    for q in range(2):
                        nb = GROUPS * (q + 1)
                        for b in range(nb):
                            g, kt = b // (q + 1), b % (q + 1)
                            last = nc.tensor.matmul(pm[:, 3, q * P:q * P + P], PJ[:, 30 + g, kt * P:kt * P + P],
                                                    probs_t(q)[:, g, kt * P:kt * P + P],
                                                    start=(b == 0), stop=(b == nb - 1))
                    last.then_inc(b_o, 1)
                take(fill)
            fill = straight([(BY["gates_b0"], from_buf(act_b), None)])
            for h in range(SLOTS):
                take(fill, 3)
                pe.wait_ge(y_high, 20 + h)
                pe.wait_ge(epi_done, BY["stick"].unit0 + 6 + 2)
                for q in range(2):
                    last = nc.tensor.transpose(pm[:, 2, q * P:q * P + P], G[:, 8 + h, q * P:q * P + P], ident)
                last.then_inc(s_z, 1)
                pe.wait_ge(s_abs, 2 * h + 1)
                nc.tensor.matmul(pm[:, 0, 0:S], G[:, 4 + h, 0:P], PJ[:, 20, :], start=True, stop=True)
                nc.tensor.matmul(pm[:, 0, S:S + P], G[:, 4 + h, P:S], PJ[:, 20, P:S], start=True,
                                 stop=True).then_inc(s_z, 1)
                take(fill, 3)
                pe.wait_ge(s_ln, h + 1)
                nc.tensor.matmul(pm[:, 1, 0:S], later, PJ[:, 22, :], start=True, stop=False,
                                 skip_group_check=True)
                nc.tensor.matmul(pm[:, 1, P:S], ones, PJ[:, 23, 0:P], start=False, stop=True,
                                 skip_group_check=True)
                nc.tensor.matmul(pm[:, 1, S:S + P], later, PJ[:, 23, 0:P], start=True, stop=True,
                                 skip_group_check=True).then_inc(s_suf, 1)
                take(fill, 2)
                pe.wait_ge(s_w, h + 1)
                nc.tensor.matmul(pm[:, 2, 0:S], PJ[:, 21, 0:P], PJ[:, 26, :], start=True, stop=False,
                                 skip_group_check=True)
                nc.tensor.matmul(pm[:, 2, P:S], PJ[:, 21, P:S], PJ[:, 27, 0:P], start=False, stop=True,
                                 skip_group_check=True).then_inc(s_o, 1)
            take(fill)

            for half in range(2):
                if half:
                    units(BY["gates_b1"], from_buf(act_b))

                def need_y2(i, j, s):
                    pe.wait_ge(y_done, 24)
                units(BY[f"mix_b{half}"], lambda i, j, k: act_a[:, 4 * (j % 2) + k, :], need_y2)

            def need_m2(i, j, s):
                if s < 2:
                    pe.wait_ge(m_low, 12 + 4 * (s + 1))
                else:
                    pe.wait_ge(epi_done, BY["mix_b1"].unit0 + 8 + 2)
            units(BY["w_out2"], from_buf(act_b), need_m2)

            def need_p(i, j, s):
                pe.wait_ge(p_low, 1)
            fill = straight([(BY["ple"], lambda i, j, k: act_a[:, 14 + k, :], need_p)])
            take(fill, 4)
            ssq(3, sq_added, BY["w_out2"].count0["sq_added"] + 8 + 2)
            take(fill)

            def need_pn(first):
                def need(i, j, s):
                    pe.wait_ge(pn_low, first + 4 * (s + 1))
                return need
            for g in range(3):
                if g == 0:
                    units(BY["ffn_up0"], from_buf(act_a), need_pn(0), lambda: ssq(4, pn_added, 8))
                else:
                    units(BY[f"ffn_up{g}"], from_buf(act_a))
                units(BY[f"ffn_down{g}"], from_buf(act_b), after_phase(f"ffn_up{g}"))
            ssq(5, sq_added, BY["ffn_down2"].count0["sq_added"] + 8 + 2)
            units(BY["ple_gate"], from_buf(act_a), need_pn(16))

        @block.scalar
        def _(act):
            def link(ins):
                chain["act"] += 1
                ins.then_inc(act_chain, 1)
                act.wait_ge(act_chain, chain["act"])

            def piece(ph, i, j, s):
                kn = 2 if ph.name == "ple" else 4
                n, at = piece_no(ph, i, j, s), slot(ph, j, s)
                body_rounds = ph.U * ph.ppu // RING
                rnd = i * body_rounds + (ph.piece0 + j * ph.ppu + s) // RING + 1
                act.wait_ge(raw_full[at], rnd * 16)
                act.wait_ge(w_used, n + 1)
                nc.scalar.copy(wh[:, at, 0:kn * S], raw[:, at, 0:kn * S]).then_inc(high_ready, 1)

            def pieces(ph, i, j):
                for s in range(ph.ppu):
                    piece(ph, i, j, s)

            def apart():
                act.sem_inc(act_gate, 1)

            def epilogue(ph, i, j):
                k, g, n = ph.kind, bank(ph, j), unit_no(ph, i, j)
                act.wait_ge(w_used, end_piece(ph, i, j))
                act.wait_ge(summed, n + 1)
                nc.scalar.copy(bcopy[:, g], ps[:, g, :, S:2 * S]).then_inc(b_copied, 1)
                t0 = dst_tile(ph, i, j)
                if k == "gate":
                    act.wait_ge(scaled, after("scaled", ph, i, j))
                    act.wait_ge(epi_done, n + 2)
                    apart()
                    nc.scalar.activation(gate_tiles(ph, t0), summ[:, g], ACT.Sigmoid).then_inc(epi_done, 1)
                elif k == "resid":
                    gain = "g_mlp" if ph.name == "w_out" else "g_mix_pre2"
                    act.wait_ge(merged, after("merged", ph, i, j))
                    apart()
                    for t in range(2):
                        last = nc.scalar.activation(tile(act_b, t0 + t)[:, 0:S], tile(PJ, t0 + t), ACT.Copy,
                                                    scale=pcol(gain, t0 + t))
                    last.then_inc(high_out, 1)
                    square(tiles(PJ, t0, 2), g, after("squared", ph, i, j))
                elif k == "up":
                    act.wait_ge(acted, after("acted", ph, i, j))
                    apart()
                    nc.scalar.copy(tiles(act_a, t0, 2)[:, :, 0:S], summ[:, g]).then_inc(high_out, 1)
                elif k in ("mix", "accsq"):
                    if k == "mix":
                        act.wait_ge(epi_done, n + 1 + 2)
                    else:
                        act.wait_ge(merged, after("merged", ph, i, j))
                    square(tiles(PJ, t0 + 16, 2), g, after("squared", ph, i, j))
                elif k == "final":
                    act.wait_ge(summed, n + 1 + 2)
                    nc.scalar.activation(summ[:, g], summ[:, g], ACT.Sigmoid).then_inc(acted, 1)

            def stages(ph, i, j):
                k, g, n = ph.kind, bank(ph, j), unit_no(ph, i, j)
                t0 = dst_tile(ph, i, j)

                def high_merged():
                    buf = act_a if k == "branch4s" else act_b
                    act.wait_ge(merged, after("merged", ph, i, j))
                    apart()
                    nc.scalar.copy(tiles(buf, t0, 2)[:, :, 0:S], tiles(PJ, t0 + 16, 2)).then_inc(high_out, 1)
                if (k == "branch4s" and j == 3) or (k == "branch2s" and j % 2 == 1):
                    return [lambda: epilogue(ph, i, j), high_merged]
                if k != "upconv":
                    return [lambda: epilogue(ph, i, j)]

                def base():
                    act.wait_ge(scaled, after("scaled", ph, i, j))
                    if j == 0:
                        act.wait_ge(epi_done, n + 2)
                    c0 = i * 2 + (16 * ph.group + 44 * j)
                    apart()
                    for t in range(2):
                        last = nc.scalar.activation(G[:, 28 + 2 * j + t, :], summ[:, g, t], ACT.Identity,
                                                    scale=pcol("conv_w2", c0 + t + 176), bias=pcol("conv_b2", c0 + t))
                    last.then_inc(conv_base, 1)

                def end():
                    act.wait_ge(acted, after("acted", ph, i, j))
                    if j == 0:
                        act.wait_ge(epi_done, n + 2)
                        nc.scalar.activation(G[:, 28:30, :], G[:, 28:30, :], ACT.Gelu_apprx_tanh).then_inc(epi_done, 1)
                    else:
                        apart()
                        nc.scalar.copy(tiles(act_b, t0, 2)[:, :, 0:S], G[:, 30:32, :]).then_inc(high_out, 1)
                return [lambda: epilogue(ph, i, j), base, lambda: None, end]

            def square(src, g, value):
                act.wait_ge(sq_added, value)
                apart()
                nc.scalar.activation(sqt[:, g], src, ACT.Square).then_inc(squared, 1)

            def rms(n):
                act.wait_ge(ssq_ready, n + 1)
                if n:
                    act.wait_ge(rstd_ready, n)
                nc.scalar.activation(rms_t, pm[:, 3, 0:S], ACT.Sqrt, scale=1.0 / D, bias=eps_t).then_inc(rms_ready, 1)

            rms_t = rms_buf[:]
            eps_t = stat[:, 64:65]

            act.wait_ge(in_par, 16)
            for b in range(8):
                act.wait_ge(in_x[b // 2], 16)
                if b >= 2:
                    act.wait_ge(sq0_added, b - 1)
                nc.scalar.activation(sqt[:, b % 2], tiles(G, 2 * b, 2), ACT.Square).then_inc(sq0_ready, 1)
                for t in range(2):
                    last = nc.scalar.activation(act_a[:, 2 * b + t, 0:S], G[:, 2 * b + t, :], ACT.Copy,
                                                scale=pcol("g_mix", 2 * b + t))
                last.then_inc(hi0, 1)
                if b % 2:
                    piece(BY["proj_a"], 0, 0, b // 2)
            act.wait_ge(zeroed, 1)
            pend = None
            pend = skewed(act, None, BY["proj_a"], pieces, epilogue, True, once=lambda: rms(0))
            ended = []
            fill = fed(pend, [BY["proj_b"], BY["gates_a0"], BY["gates_a1"]], piece, epilogue, ended)
            take(fill, 4)

            lam = par[:, COL["lru_lambda"]:COL["lru_lambda"] + 4]
            link(nc.scalar.activation(stat[:, 0:4], lam, ACT.Abs))
            link(nc.scalar.activation(stat[:, 4:8], stat[:, 0:4], ACT.Exp, scale=-1.0))
            nc.scalar.activation(stat[:, 8:12], stat[:, 4:8], ACT.Ln, bias=1.0).then_inc(sp_exp, 1)
            act.wait_ge(f_biased, 1)
            link(nc.scalar.activation(G[0:HEADS, 30, :], PJ[0:HEADS, 32, :], ACT.Abs))
            link(nc.scalar.activation(G[0:HEADS, 30, :], G[0:HEADS, 30, :], ACT.Exp, scale=-1.0))
            nc.scalar.activation(G[0:HEADS, 30, :], G[0:HEADS, 30, :], ACT.Ln, bias=1.0).then_inc(f_log, 1)
            act.wait_ge(nscale_ready, 1)
            for c in range(BT):
                if c:
                    act.wait_ge(y_done, 3 * c)
                nc.scalar.activation(tile(G, 16), PJ[:, c, :], ACT.Identity, scale=pcol("lru_conv_w", 12 + c),
                                     bias=pcol("lru_conv_b", c)).then_inc(lru_base, 1)
                act.wait_ge(sc_z, c + 1)
                nc.scalar.activation(tile(G, 28), tile(G, 27), ACT.Copy,
                                     scale=pcol("sconv_w", 8 + c)).then_inc(sc_base, 1)
                take(fill, 2)
                act.wait_ge(lru_ps, c + 1)
                nc.scalar.activation(tile(G, 17), pm[:, 1, 0:S], ACT.Sigmoid, bias=pcol("lru_br", c))
                nc.scalar.activation(tile(G, 18), pm[:, 1, S:2 * S], ACT.Sigmoid,
                                     bias=pcol("lru_bi", c)).then_inc(lru_act, 1)
                act.wait_ge(lru_act, c + 1)
                nc.scalar.activation(tile(G, 19), tile(G, 17), ACT.Exp, scale=stat[:, 12 + c:13 + c])
                nc.scalar.activation(tile(G, 20), tile(G, 17), ACT.Tanh,
                                     scale=stat[:, 12 + c:13 + c]).then_inc(lru_pre, 1)
                act.wait_ge(pool_ps, c + 1)
                nc.scalar.activation(tile(G, 26), pm[:, 2, 0:S], ACT.Copy,
                                     scale=pcol("pool_scale", c)).then_inc(pool_y, 1)
                take(fill, 2)
                act.wait_ge(lru_sqrt, 2 * c + 1)
                nc.scalar.activation(tile(G, 21), tile(G, 21), ACT.Sqrt).then_inc(lru_sqrt, 1)
                take(fill, 2)
                act.wait_ge(lru_h, c + 1)
                nc.scalar.copy(act_b[:, c, 0:S], tile(G, 22)).then_inc(y_high, 1)
                act.wait_ge(pool_y, c + 1)
                nc.scalar.copy(act_b[:, 4 + c, 0:S], tile(G, 26)).then_inc(y_high, 1)
                act.wait_ge(sc_y, c + 1)
                nc.scalar.copy(act_b[:, 8 + c, 0:S], tile(G, 28)).then_inc(y_high, 1)
            act.wait_ge(y_done, 12)
            for c in range(BT):
                act.wait_ge(epi_done, BY["proj_b"].unit0 + 2 + 6)
                nc.scalar.activation(G[:, 16, :], PJ[:, 20 + c, :], ACT.Square)
                nc.scalar.activation(G[:, 17, :], PJ[:, 24 + c, :], ACT.Square).then_inc(at_sq, 1)
                take(fill, 2)
                act.wait_ge(at_ssq, c + 1)
                if c:
                    act.wait_ge(at_qk, c)
                nc.scalar.activation(G[:, 18:20, :].rearrange("p o n -> p (o n)"), pm[:, 0, :], ACT.Sqrt,
                                     scale=1.0 / HD, bias=eps_t).then_inc(at_rms, 1)
                take(fill, 6)
                act.wait_ge(at_max, c + 1)
                sv = flat3(G, 26)
                for e in range(2):
                    nc.scalar.activation(sv[:, e, 0:P], sv[:, e, 0:P], ACT.Exp, bias=stat[:, 36 + e:37 + e],
                                         accum_out=stat[:, 40 + e:41 + e])
                    last = nc.scalar.activation(sv[:, e, P:3 * P], sv[:, e, P:3 * P], ACT.Exp,
                                                bias=stat[:, 38 + e:39 + e], accum_out=stat[:, 42 + e:43 + e])
                last.then_inc(at_exp, 1)
                act.wait_ge(at_ri, c + 1)
                for e in range(2):
                    nc.scalar.activation(sv[:, e, 0:P], sv[:, e, 0:P], ACT.Copy, scale=stat[:, 60 + e:61 + e])
                    last = nc.scalar.activation(sv[:, e, P:3 * P], sv[:, e, P:3 * P], ACT.Copy,
                                                scale=stat[:, 62 + e:63 + e])
                last.then_inc(at_p, 1)
                take(fill, 8)
                act.wait_ge(at_o, c + 1)
                link(nc.scalar.copy(G[:, 23, :], pm[:, 0, 0:S]))
                nc.scalar.copy(act_b[:, 12 + c, 0:S], G[:, 23, :]).then_inc(y_high, 1)
            take(fill)
            pend = ended.pop()

            def one(pend, ph, started=False, once=None):
                if ph.kind.startswith("branch") or ph.kind in ("upconv", "store") and ph.name != "ffn_down0":
                    return threaded(act, pend, ph, piece, stages, started, once)
                return skewed(act, pend, ph, pieces, epilogue, started, once)

            def phases(names, pend):
                for n in names:
                    pend = one(pend, BY[n])
                return pend

            def merge_phases(names, pend, last_gates, buf, n):
                pend = phases(names, pend)
                gates = BY[last_gates]

                def merged_high():
                    act.wait_ge(w_used, end_piece(gates, gates.bodies - 1, gates.U - 1))
                    for t in range(n):
                        nc.scalar.copy(buf[:, t, 0:S], PJ[:, 16 + t, :]).then_inc(m_high, 1)
                return one(pend, BY[names_last(names)], False, merged_high)

            def names_last(names):
                return names[-1].replace("gates", "mix")

            def skip_first(ph, once=None):
                return one(None, ph, True, once)

            pend = merge_phases(MERGE_A, pend, "gates_a3", act_a, 12)
            pend = phases(["w_out"], pend)
            pieces(BY["mlp_up0"], 0, 0)
            pend()
            pend = skip_first(BY["mlp_up0"], lambda: rms(1))
            pend = phases(["mlp_down0", "mlp_up1", "mlp_down1", "mlp_up2", "mlp_down2", "mlp_up3", "mlp_down3"], pend)
            pieces(BY["slots0"], 0, 0)
            pend()
            pend = skip_first(BY["slots0"], lambda: rms(2))
            pend = phases(["slots0_end"], pend)
            for half in range(2):
                names, f = ((["slots1", "slots1_end"], (7, 11)), (["stick"], (5, 7)))[half]
                ended = []
                fill = fed(pend, [BY[x] for x in names], piece, epilogue, ended)
                take(fill, 4)
                for e in range(2):
                    h = 2 * half + e
                    take(fill, f[0])
                    act.wait_ge(b_max, h + 1)
                    nc.scalar.activation(probs(0), probs(0), ACT.Exp, bias=stat[:, 36:37], accum_out=stat[:, 38:39])
                    nc.scalar.activation(probs(1), probs(1), ACT.Exp, bias=stat[:, 37:38],
                                         accum_out=stat[:, 39:40]).then_inc(b_exp, 1)
                    act.wait_ge(b_ri, h + 1)
                    nc.scalar.activation(probs(0), probs(0), ACT.Copy, scale=stat[:, 40:41])
                    nc.scalar.activation(probs(1), probs(1), ACT.Copy, scale=stat[:, 41:42]).then_inc(b_p, 1)
                    take(fill, f[1])
                    act.wait_ge(b_o, h + 1)
                    link(nc.scalar.copy(PJ[:, 25, :], pm[:, 3, 0:S]))
                    nc.scalar.copy(act_a[:, h, 0:S], PJ[:, 25, :]).then_inc(y_high, 1)
                take(fill)
                pend = ended.pop()
            ended = []
            fill = fed(pend, [BY["gates_b0"]], piece, epilogue, ended)
            take(fill, 4)
            for h in range(SLOTS):
                take(fill, 3)
                act.wait_ge(s_abs, 2 * h + 2)
                z3, l3, w3 = zview(PJ, 24), zview(PJ, 22), zview(PJ, 26)
                link(nc.scalar.activation(l3, z3, ACT.Abs))
                link(nc.scalar.activation(l3, l3, ACT.Exp, scale=-1.0))
                nc.scalar.activation(l3, l3, ACT.Ln, bias=1.0).then_inc(s_lnb, 1)
                take(fill, 3)
                act.wait_ge(s_logw, h + 1)
                nc.scalar.activation(w3, w3, ACT.Exp).then_inc(s_w, 1)
                take(fill, 2)
                act.wait_ge(s_o, h + 1)
                act.wait_ge(y_done, 20 + h)
                link(nc.scalar.copy(PJ[:, 28, :], pm[:, 2, 0:S]))
                nc.scalar.copy(act_a[:, 4 + h, 0:S], PJ[:, 28, :]).then_inc(y_high, 1)
            take(fill)
            pend = merge_phases(MERGE_B, ended.pop(), "gates_b1", act_b, 8)
            act.wait_ge(in_p, 16)
            nc.scalar.copy(act_a[:, 14:16, 0:S], PJ[:, 32:34, :]).then_inc(p_high, 1)
            pend = phases(["w_out2"], pend)
            fill = fed(pend, [BY["ple"]], piece, epilogue, ended)
            take(fill, 5)

            def beside(b):
                if b < 3:
                    take(fill, 1)
                elif b == 3:
                    take(fill)
                    ended.pop()()
                elif b < 8:
                    piece(BY["ffn_up0"], 0, 0, b - 4)

            def post_norm(n, first, gain, squares, beside=None):
                rms(n)
                for b in range(8):
                    if beside:
                        beside(b)
                    if b == 7 and squares:
                        act.wait_ge(w_used, end_piece(BY["ple"], 1, 3))
                    act.wait_ge(pn_r, first // 2 + b + 1)
                    for t in range(2):
                        k = 2 * b + t
                        if gain:
                            nc.scalar.activation(act_a[:, k, 0:S], PJ[:, k, :], ACT.Copy,
                                                 scale=pcol(gain, k)).then_inc(pn_high, 1)
                        else:
                            nc.scalar.copy(act_a[:, k, 0:S], PJ[:, k, :]).then_inc(pn_high, 1)
                    if squares:
                        if b >= 2:
                            act.wait_ge(pn_added, b - 1)
                        nc.scalar.activation(sqt[:, b % 2], PJ[:, 2 * b:2 * b + 2, :], ACT.Square).then_inc(pn_sq, 1)
            post_norm(3, 0, "g_ffn_pre2", True, beside)
            pend = skip_first(BY["ffn_up0"], lambda: rms(4))
            pend = phases(["ffn_down0", "ffn_up1", "ffn_down1", "ffn_up2", "ffn_down2"], pend)
            pieces(BY["ple_gate"], 0, 0)
            pend()
            post_norm(5, 16, None, False)
            pend = skip_first(BY["ple_gate"])
            pend()

        @block.vector
        def _(dve):
            def link(ins):
                chain["dve"] += 1
                ins.then_inc(dve_chain, 1)
                dve.wait_ge(dve_chain, chain["dve"])

            def piece(ph, i, j, s):
                kn = 2 if ph.name == "ple" else 4
                n, at = piece_no(ph, i, j, s), slot(ph, j, s)
                dve.wait_ge(high_ready, n + 1)
                nc.vector.tensor_tensor(wl[:, at, 0:kn * S], raw[:, at, 0:kn * S],
                                        wh[:, at, 0:kn * S].bitcast(F32), ALU.subtract).then_inc(split_done, 1)

            def pieces(ph, i, j):
                for s in range(ph.ppu):
                    piece(ph, i, j, s)

            def low(dst, src, inc):
                nc.vector.tensor_tensor(dst[:, :, S:2 * S], src, dst[:, :, 0:S].bitcast(F32), ALU.subtract).then_inc(inc, 1)

            def epilogue(ph, i, j):
                k, g, n = ph.kind, bank(ph, j), unit_no(ph, i, j)
                t0 = dst_tile(ph, i, j)
                A_half = ps[:, g, :, 0:S]
                s2 = summ[:, g]
                dve.wait_ge(b_copied, n + 1)
                dve.wait_ge(epi_done, n + 1)
                if k in ("mix", "store"):
                    dst = tiles(G, t0, 2) if ph.name == "ple" else tiles(PJ, t0 + 16, 2)
                    nc.vector.tensor_tensor(dst, A_half, bcopy[:, g], ALU.add).then_inc(summed, 1)
                    dve.wait_ge(summed, n + 1 + 2)
                    dve.wait_ge(epi_done, n + 2)
                    dve.sem_inc(epi_done, 1)
                    return
                nc.vector.tensor_tensor(s2, A_half, bcopy[:, g], ALU.add).then_inc(summed, 1)
                if k in ("proj", "gate", "up", "upconv"):
                    dve.wait_ge(summed, n + 1 + 2)
                    r2 = rstd[:].unsqueeze(1).to_broadcast([P, 2, S])
                    if k == "proj":
                        dst = proj_tiles(ph, t0)
                        dve.wait_ge(epi_done, n + 2)
                        nc.vector.tensor_tensor(dst, s2, r2, ALU.mult).then_inc(epi_done, 1)
                        return
                    nc.vector.tensor_tensor(s2, s2, r2, ALU.mult).then_inc(scaled, 1)
                if k == "resid":
                    gain = "g_mlp" if ph.name == "w_out" else "g_mix_pre2"
                    dve.wait_ge(high_out, after("high_out", ph, i, j))
                    dve.wait_ge(epi_done, n + 2)
                    for t in range(2):
                        d = tile(act_b, t0 + t)
                        last = nc.vector.scalar_tensor_tensor(out=d[:, S:2 * S], in0=tile(PJ, t0 + t),
                                                              scalar=pcol(gain, t0 + t), in1=d[:, 0:S].bitcast(F32),
                                                              op0=ALU.mult, op1=ALU.subtract)
                    last.then_inc(epi_done, 1)
                elif k == "up":
                    dve.wait_ge(scaled, after("scaled", ph, i, j))
                    nc.vector.scalar_tensor_tensor(out=s2, in0=s2, scalar=0.0, in1=s2, op0=ALU.max,
                                                   op1=ALU.mult).then_inc(acted, 1)
                    dve.wait_ge(high_out, after("high_out", ph, i, j))
                    dve.wait_ge(epi_done, n + 2)
                    low(tiles(act_a, t0, 2), s2, epi_done)
                elif k == "final":
                    dve.wait_ge(acted, after("acted", ph, i, j))
                    nc.vector.tensor_tensor(s2, s2, tiles(G, t0, 2), ALU.mult).then_inc(scaled, 1)

            def stages(ph, i, j):
                k, g, n = ph.kind, bank(ph, j), unit_no(ph, i, j)
                t0 = dst_tile(ph, i, j)
                s2 = summ[:, g]

                def total():
                    epilogue(ph, i, j)

                def gated():
                    nb = 4 if k.startswith("branch4") else 2
                    br = j % nb
                    gate = gate_tiles(ph, i * 2 + 4 * br) if nb == 4 else tiles(G, i * 4 + (12 + 8 * br + 2 * (j // 2)), 2)
                    dve.wait_ge(summed, n + 1 + 2)
                    if br == 0:
                        dve.wait_ge(epi_done, n + 2)
                        nc.vector.tensor_tensor(tiles(PJ, t0 + 16, 2), s2, gate, ALU.mult).then_inc(epi_done, 1)
                    else:
                        nc.vector.tensor_tensor(s2, s2, gate, ALU.mult).then_inc(scaled, 1)
                        if br == nb - 1 and k.endswith("s"):
                            dve.wait_ge(high_out, after("high_out", ph, i, j))
                            low(tiles(act_a if nb == 4 else act_b, t0, 2), tiles(PJ, t0 + 16, 2), epi_done)

                c0 = i * 2 + (16 * ph.group + 44 * j)
                y = G[:, 28 + 2 * (j % 2):30 + 2 * (j % 2), :]

                def taps():
                    dve.wait_ge(conv_base, after("conv_base", ph, i, j))
                    for tap in (1, 0):
                        sh = 2 - tap
                        for t in range(2):
                            last = nc.vector.scalar_tensor_tensor(
                                out=y[:, t, sh:S], in0=summ[:, g, t, 0:S - sh],
                                scalar=pcol("conv_w2", c0 + t + 88 * tap), in1=y[:, t, sh:S],
                                op0=ALU.mult, op1=ALU.add)
                            if tap:
                                last.then_inc(conv_tap, 1)
                        if tap:
                            dve.wait_ge(conv_tap, after("conv_tap", ph, i, j))
                    last.then_inc(acted if j == 0 else conv_done, 1)

                def product():
                    if j:
                        dve.wait_ge(conv_done, after("conv_done", ph, i, j))
                        dve.wait_ge(epi_done, n + 2)
                        nc.vector.tensor_tensor(G[:, 30:32, :], G[:, 28:30, :], G[:, 30:32, :],
                                                ALU.mult).then_inc(acted, 1)

                def rest():
                    if j:
                        dve.wait_ge(high_out, after("high_out", ph, i, j))
                        low(tiles(act_b, t0, 2), G[:, 30:32, :], epi_done)
                if k == "upconv":
                    return [total, taps, product, rest]
                return [total, gated] if k.startswith("branch") else [total]

            def recip(n):
                dve.wait_ge(rms_ready, n + 1)
                nc.vector.reciprocal(rstd[:], rms_buf[:]).then_inc(rstd_ready, 1)
                dve.wait_ge(rstd_ready, n + 1)

            dve.sem_inc(summed, 2)
            dve.sem_inc(epi_done, 2)
            nc.vector.memset(stat[:, 64:65], EPS).then_inc(zeroed, 1)
            dve.wait_ge(in_par, 16)
            for b in range(8):
                dve.wait_ge(hi0, b + 1)
                for t in range(2):
                    k = 2 * b + t
                    last = nc.vector.scalar_tensor_tensor(out=act_a[:, k, S:2 * S], in0=G[:, k, :],
                                                          scalar=pcol("g_mix", k), in1=act_a[:, k, 0:S].bitcast(F32),
                                                          op0=ALU.mult, op1=ALU.subtract)
                last.then_inc(lo0, 1)
                if b % 2:
                    piece(BY["proj_a"], 0, 0, b // 2)

            def one(pend, ph, started=False, once=None):
                if ph.kind.startswith("branch") or ph.kind in ("upconv", "store") and ph.name != "ffn_down0":
                    return threaded(dve, pend, ph, piece, stages, started, once)
                return skewed(dve, pend, ph, pieces, epilogue, started, once)

            def skip_first(ph, once=None):
                return one(None, ph, True, once)

            def phases(names, pend):
                for n in names:
                    pend = one(pend, BY[n])
                return pend

            pend = skewed(dve, None, BY["proj_a"], pieces, epilogue, True, once=lambda: recip(0))
            ended = []
            fill = fed(pend, [BY["proj_b"], BY["gates_a0"], BY["gates_a1"]], piece, epilogue, ended)
            take(fill, 4)
            dve.wait_ge(epi_done, BY["proj_b"].unit0 + 2)

            dve.wait_ge(in_c1, 21 * 16)
            link(nc.vector.memset(onesrow, 1.0))
            lam = par[:, COL["lru_lambda"]:COL["lru_lambda"] + 4]
            link(nc.vector.tensor_scalar(stat[:, 16:20], lam, -1.0, 0.0, ALU.mult, ALU.max))
            dve.wait_ge(sp_exp, 1)
            link(nc.vector.tensor_tensor(stat[:, 16:20], stat[:, 16:20], stat[:, 8:12], ALU.add))
            nc.vector.tensor_scalar(stat[:, 12:16], stat[:, 16:20], -8.0, None, ALU.mult)
            nc.vector.tensor_scalar(stat[:, 20:21], pcol("q_g"), HD ** -0.5, None, ALU.mult).then_inc(nscale_ready, 1)
            dve.wait_ge(f_logits, 1)
            link(nc.vector.tensor_tensor(PJ[0:HEADS, 32, :], pm[0:HEADS, 0, 0:S], rstd[0:HEADS, :], ALU.mult))
            nc.vector.tensor_scalar(PJ[0:HEADS, 32, :], PJ[0:HEADS, 32, :], par[0:HEADS, COL["forget_b"]:COL["forget_b"] + 1],
                                    None, ALU.add).then_inc(f_biased, 1)
            dve.wait_ge(f_log, 1)
            link(nc.vector.scalar_tensor_tensor(out=G[0:HEADS, 31, :], in0=PJ[0:HEADS, 32, :], scalar=0.0,
                                                in1=G[0:HEADS, 30, :], op0=ALU.min, op1=ALU.subtract))
            link(nc.vector.tensor_tensor_scan(PJ[0:HEADS, 32, :], G[0:HEADS, 12, :], G[0:HEADS, 31, :], 0.0,
                                              ALU.mult, ALU.add))
            nc.vector.tensor_scalar(PJ[0:HEADS, 33, :], PJ[0:HEADS, 32, :], -1.0, None, ALU.mult).then_inc(cum_ready, 1)

            for c in range(BT):
                xa = PJ[:, c, :]
                if c:
                    dve.wait_ge(y_done, 3 * c)
                link(nc.vector.tensor_tensor(tile(G, 27), PJ[:, 12 + c, :], PJ[:, 16 + c, :], ALU.mult))
                dve.sem_inc(sc_z, 1)
                u = tile(G, 16)
                dve.wait_ge(lru_base, c + 1)
                for tap in (2, 1, 0):
                    sh = 3 - tap
                    nc.vector.scalar_tensor_tensor(out=u[:, sh:S], in0=xa[:, 0:S - sh],
                                                   scalar=pcol("lru_conv_w", 4 * tap + c), in1=u[:, sh:S],
                                                   op0=ALU.mult, op1=ALU.add).then_inc(lru_u, 1)
                    dve.wait_ge(lru_u, 3 * c + 3 - tap)
                take(fill, 1)
                dve.wait_ge(win_ready, c + 1)
                win = 2 << c
                src = tile(G, 23 + c % 2)
                xp = PJ[:, 4 + c, :]
                pw = tile(G, 25)
                link(nc.vector.scalar_tensor_tensor(out=pw, in0=src, scalar=1.0 / win, in1=xp, op0=ALU.mult,
                                                    op1=ALU.subtract))
                link(nc.vector.tensor_tensor(stat[:, 44:44 + win], src[:, 0:win], inv16[:, 0:win], ALU.mult))
                nc.vector.tensor_tensor(pw[:, 0:win], stat[:, 44:44 + win], xp[:, 0:win],
                                        ALU.subtract).then_inc(pooled, 1)
                take(fill, 1)
                y = tile(G, 28)
                z = tile(G, 27)
                dve.wait_ge(sc_base, c + 1)
                for tap in (1, 0):
                    sh = 2 - tap
                    link(nc.vector.scalar_tensor_tensor(out=y[:, sh:S], in0=z[:, 0:S - sh],
                                                        scalar=pcol("sconv_w", 4 * tap + c), in1=y[:, sh:S],
                                                        op0=ALU.mult, op1=ALU.add))
                nc.vector.tensor_tensor(y, y, PJ[:, 8 + c, :], ALU.mult).then_inc(sc_y, 1)
                take(fill, 1)
                dve.wait_ge(lru_pre, c + 1)
                v = tile(G, 21)
                link(nc.vector.tensor_tensor(v, tile(G, 19), tile(G, 19), ALU.mult))
                link(nc.vector.scalar_tensor_tensor(out=v, in0=v, scalar=1.0, in1=tile(G, 20), op0=ALU.add,
                                                    op1=ALU.mult))
                nc.vector.tensor_scalar(v, v, -1.0, TINY, ALU.mult, ALU.max).then_inc(lru_sqrt, 1)
                link(nc.vector.tensor_tensor(tile(G, 18), tile(G, 18), u, ALU.mult))
                take(fill, 1)
                dve.wait_ge(lru_sqrt, 2 * c + 2)
                link(nc.vector.tensor_tensor(v, v, tile(G, 18), ALU.mult))
                nc.vector.tensor_tensor_scan(tile(G, 22), tile(G, 19), v, 0.0, ALU.mult,
                                             ALU.add).then_inc(lru_h, 1)
                take(fill, 2)
                for b, src in ((0, 22), (1, 26), (2, 28)):
                    dve.wait_ge(y_high, 3 * c + b + 1)
                    low(act_b[:, 4 * b + c:4 * b + c + 1, :], G[:, src:src + 1, :], y_done)
            dve.wait_ge(cumt_ps, 1)
            nc.vector.tensor_copy(stat[:, 44:60], pm[:, 0, 256:272]).then_inc(cumt_ready, 1)
            dve.wait_ge(cumt_ready, 1)
            for c in range(BT):
                dve.wait_ge(y_done, 12 + c)
                take(fill, 2)
                dve.wait_ge(at_vps, c + 1)
                nc.vector.tensor_copy(G[:, 22, :], pm[:, 1, 0:S]).then_inc(at_v, 1)
                dve.wait_ge(at_rms, c + 1)
                rr = G[:, 18:20, :].rearrange("p o n -> p (o n)")
                link(nc.vector.reciprocal(rr, rr))
                nc.vector.scalar_tensor_tensor(out=G[:, 20, :], in0=PJ[:, 20 + c, :], scalar=stat[:, 20:21],
                                               in1=G[:, 18, :], op0=ALU.mult, op1=ALU.mult)
                nc.vector.scalar_tensor_tensor(out=G[:, 21, :], in0=PJ[:, 24 + c, :], scalar=pcol("k_g"),
                                               in1=G[:, 19, :], op0=ALU.mult, op1=ALU.mult).then_inc(at_qk, 1)
                take(fill, 6)
                mn, sv, pt = flat3(G, 23), flat3(G, 26), flat3(G, 29)
                dve.wait_ge(at_lg, c + 1)
                nc.vector.tensor_tensor(mn[:, 0], pm[:, 1, 0:3 * P], mask3, ALU.add)
                link(nc.vector.tensor_tensor(mn[:, 1], pm[:, 0, 0:3 * P], mask3, ALU.add))
                for e in range(2):
                    h = 2 * c + e
                    nc.vector.scalar_tensor_tensor(out=sv[:, e, 0:P], in0=pm[:, 2 + e, 0:P],
                                                   scalar=stat[:, 44 + h:45 + h], in1=mn[:, e, 0:P],
                                                   op0=ALU.add, op1=ALU.add)
                    last = nc.vector.scalar_tensor_tensor(out=sv[:, e, P:3 * P], in0=pm[:, 2 + e, P:3 * P],
                                                          scalar=stat[:, 52 + h:53 + h], in1=mn[:, e, P:3 * P],
                                                          op0=ALU.add, op1=ALU.add)
                link(last)
                nc.vector.reduce_max(stat[:, 32:34], sv[:, :, 0:P], AX.X)
                link(nc.vector.reduce_max(stat[:, 34:36], sv[:, :, P:3 * P], AX.X))
                nc.vector.tensor_scalar(stat[:, 36:40], stat[:, 32:36], -1.0, None, ALU.mult).then_inc(at_max, 1)
                dve.wait_ge(at_exp, c + 1)
                nc.vector.reciprocal(stat[:, 60:64], stat[:, 40:44]).then_inc(at_ri, 1)
                take(fill, 5)
                dve.wait_ge(at_pt, c + 1)
                nc.vector.tensor_copy(pt, pm[:, 2:4, 0:3 * P]).then_inc(at_ptc, 1)
                take(fill, 3)
                dve.wait_ge(y_high, 12 + c + 1)
                low(act_b[:, 12 + c:13 + c, :], G[:, 23:24, :], y_done)
            take(fill)
            pend = ended.pop()

            def merge_phases(names, pend, buf, first, n):
                pend = phases(names, pend)

                def merged_low():
                    for t in range(n):
                        dve.wait_ge(m_high, first + t + 1)
                        low(buf[:, t:t + 1, :], PJ[:, 16 + t:17 + t, :], m_low)
                return one(pend, BY[names[-1].replace("gates", "mix")], False, merged_low)

            pend = merge_phases(MERGE_A, pend, act_a, 0, 12)
            pend = phases(["w_out"], pend)
            pieces(BY["mlp_up0"], 0, 0)
            pend()
            pend = skip_first(BY["mlp_up0"], lambda: recip(1))
            pend = phases(["mlp_down0", "mlp_up1", "mlp_down1", "mlp_up2", "mlp_down2", "mlp_up3", "mlp_down3"], pend)
            pieces(BY["slots0"], 0, 0)
            pend()
            pend = skip_first(BY["slots0"], lambda: recip(2))
            pend = phases(["slots0_end"], pend)
            dve.wait_ge(in_c2, 16)
            for half in range(2):
                names, f = ((["slots1", "slots1_end"], (4, 3, 7, 4)), (["stick"], (3, 2, 4, 3)))[half]
                ended = []
                fill = fed(pend, [BY[x] for x in names], piece, epilogue, ended)
                take(fill, 4)
                dve.wait_ge(epi_done, BY[f"slots{half}_end"].unit0 + 1 + 2)
                for e in range(2):
                    h = 2 * half + e
                    if h:
                        dve.wait_ge(y_done, 16 + h)
                    for g in range(GROUPS):
                        last = nc.vector.tensor_scalar(PJ[:, 20 + g, :], slot_tile(half, 2 * g + e), HD2_SCALE, None,
                                                       ALU.mult)
                    last.then_inc(b_q, 1)
                    take(fill, f[0])
                    dve.wait_ge(b_vps, h + 1)
                    nc.vector.tensor_copy(PJ[:, 30:32, :].rearrange("p o n -> p (o n)"), pm[:, 0, :])
                    nc.vector.tensor_copy(PJ[:, 32, :], pm[:, 1, 0:S]).then_inc(b_v, 1)
                    take(fill, f[1])
                    dve.wait_ge(b_lg, h + 1)
                    for q in range(2):
                        for g in range(GROUPS):
                            last = nc.vector.scalar_tensor_tensor(
                                out=probs(q)[:, g], in0=dist[:, g, P * (1 - q):2 * P], scalar=slope(g * SLOTS + h),
                                in1=group_bank(q, g), op0=ALU.mult, op1=ALU.add)
                    link(last)
                    nc.vector.tensor_reduce(stat[:, 32:33], probs(0), AX.XY, ALU.max)
                    link(nc.vector.tensor_reduce(stat[:, 33:34], probs(1), AX.XY, ALU.max))
                    nc.vector.tensor_scalar(stat[:, 36:38], stat[:, 32:34], -1.0, None, ALU.mult).then_inc(b_max, 1)
                    dve.wait_ge(b_exp, h + 1)
                    nc.vector.reciprocal(stat[:, 40:42], stat[:, 38:40]).then_inc(b_ri, 1)
                    take(fill, f[2])
                    dve.wait_ge(b_pt, h + 1)
                    nc.vector.tensor_copy(probs_t(0), pm[:, 2, 0:3 * P].rearrange("p (g n) -> p g n", g=GROUPS))
                    flat = probs_t(1)
                    nc.vector.tensor_copy(flat[:, 0:2], pm[:, 0, :].rearrange("p (g n) -> p g n", g=2))
                    nc.vector.tensor_copy(flat[:, 2], pm[:, 1, 0:S]).then_inc(b_ptc, 1)
                    take(fill, f[3])
                    dve.wait_ge(y_high, 16 + h + 1)
                    low(act_a[:, h:h + 1, :], PJ[:, 25:26, :], y_done)
                take(fill)
                pend = ended.pop()
            ended = []
            fill = fed(pend, [BY["gates_b0"]], piece, epilogue, ended)
            take(fill, 4)
            dve.wait_ge(epi_done, BY["stick"].unit0 + 6 + 2)
            for h in range(SLOTS):
                dve.wait_ge(y_done, 20 + h)
                nc.vector.tensor_scalar(PJ[:, 20, :], G[:, h, :], HD2_SCALE, None, ALU.mult)
                take(fill, 2)
                dve.wait_ge(s_z, 2 * h + 1)
                nc.vector.tensor_copy(PJ[:, 21, :], pm[:, 2, 0:S]).then_inc(s_abs, 1)
                take(fill, 1)
                dve.wait_ge(s_z, 2 * h + 2)
                nc.vector.tensor_copy(zview(PJ, 24), pm[:, 0, 0:3 * P]).then_inc(s_abs, 1)
                take(fill, 1)
                dve.wait_ge(s_lnb, h + 1)
                z3, l3, w3 = zview(PJ, 24), zview(PJ, 22), zview(PJ, 26)
                link(nc.vector.scalar_tensor_tensor(out=l3, in0=z3, scalar=0.0, in1=l3, op0=ALU.max, op1=ALU.add))
                nc.vector.scalar_tensor_tensor(out=l3[:, 0:S], in0=l3[:, 0:S], scalar=-1.0, in1=before01,
                                               op0=ALU.mult, op1=ALU.mult)
                nc.vector.scalar_tensor_tensor(out=l3[:, S:3 * P], in0=l3[:, S:3 * P], scalar=-1.0,
                                               in1=before01[:, 0:P], op0=ALU.mult, op1=ALU.mult).then_inc(s_ln, 1)
                dve.wait_ge(s_ln, h + 1)
                link(nc.vector.tensor_tensor(z3, z3, l3, ALU.add))
                nc.vector.tensor_tensor(z3[:, 0:S], z3[:, 0:S], before_neg, ALU.add)
                link(nc.vector.tensor_tensor(z3[:, S:3 * P], z3[:, S:3 * P], before_neg[:, 0:P], ALU.add))
                take(fill, 2)
                dve.wait_ge(s_suf, h + 1)
                nc.vector.tensor_tensor(w3, z3, pm[:, 1, 0:3 * P], ALU.add).then_inc(s_logw, 1)
                take(fill, 2)
                dve.wait_ge(y_high, 20 + h + 1)
                low(act_a[:, 4 + h:5 + h, :], PJ[:, 28:29, :], y_done)
            take(fill)
            pend = merge_phases(MERGE_B, ended.pop(), act_b, 12, 8)
            dve.wait_ge(p_high, 1)
            low(act_a[:, 14:16, :], PJ[:, 32:34, :], p_low)
            pend = phases(["w_out2"], pend)
            fill = fed(pend, [BY["ple"]], piece, epilogue, ended)
            take(fill, 5)

            def beside(b):
                if b < 3:
                    take(fill, 1)
                elif b == 3:
                    take(fill)
                    ended.pop()()
                elif b < 8:
                    piece(BY["ffn_up0"], 0, 0, b - 4)

            def post_norm(n, first, post, gain, beside=None):
                recip(n)
                for b in range(9):
                    if b < 8:
                        if b >= 2:
                            dve.wait_ge(pn_r, first // 2 + b - 1)
                        for t in range(2):
                            k = 2 * b + t
                            last = nc.vector.scalar_tensor_tensor(out=summ[:, b % 2, t], in0=PJ[:, 16 + k, :],
                                                                  scalar=pcol(post, k), in1=rstd[:],
                                                                  op0=ALU.mult, op1=ALU.mult)
                        last.then_inc(pn_t, 1)
                    if beside:
                        beside(b)
                    if b:
                        for t in range(2):
                            k = 2 * (b - 1) + t
                            dve.wait_ge(pn_high, first + k + 1)
                            if gain:
                                nc.vector.scalar_tensor_tensor(
                                    out=act_a[:, k, S:2 * S], in0=PJ[:, k, :], scalar=pcol(gain, k),
                                    in1=act_a[:, k, 0:S].bitcast(F32), op0=ALU.mult,
                                    op1=ALU.subtract).then_inc(pn_low, 1)
                            else:
                                nc.vector.tensor_tensor(act_a[:, k, S:2 * S], PJ[:, k, :],
                                                        act_a[:, k, 0:S].bitcast(F32),
                                                        ALU.subtract).then_inc(pn_low, 1)
            dve.wait_ge(epi_done, BY["ple"].unit0 + 2)
            post_norm(3, 0, "g_mix_post2", "g_ffn_pre2", beside)
            dve.wait_ge(pn_r, 8)
            pend = skip_first(BY["ffn_up0"], lambda: recip(4))
            pend = phases(["ffn_down0", "ffn_up1", "ffn_down1", "ffn_up2", "ffn_down2"], pend)
            pieces(BY["ple_gate"], 0, 0)
            pend()
            dve.wait_ge(epi_done, BY["ple_gate"].unit0 + 2)
            post_norm(5, 16, "g_ffn_post2", None)
            dve.wait_ge(pn_r, 16)
            pend = skip_first(BY["ple_gate"])
            pend()

        @block.gpsimd
        def _(pool):
            def link(ins):
                chain["pool"] += 1
                ins.then_inc(pool_chain, 1)
                pool.wait_ge(pool_chain, chain["pool"])

            def add_square(g, wait, value, inc):
                pool.wait_ge(wait, value)
                nc.gpsimd.tensor_tensor(sqacc[:], sqacc[:], sqt[:, g], ALU.add).then_inc(inc, 1)

            def apart():
                pool.sem_inc(pool_gate, 1)

            def epilogue(ph, i, j):
                k, g, n = ph.kind, bank(ph, j), unit_no(ph, i, j)
                t0 = dst_tile(ph, i, j)
                s2 = summ[:, g]
                if k.startswith("branch"):
                    nb = 4 if k.startswith("branch4") else 2
                    if j % nb:
                        pool.wait_ge(scaled, after("scaled", ph, i, j))
                        pool.wait_ge(epi_done, n + 2)
                        d = tiles(PJ, t0 + 16, 2)
                        split = j % nb == nb - 1 and k.endswith("s")
                        apart()
                        nc.gpsimd.tensor_tensor(d, d, s2, ALU.add).then_inc(merged if split else epi_done, 1)
                elif k == "resid":
                    pool.wait_ge(summed, n + 1 + 2)
                    d = tiles(PJ, t0, 2)
                    apart()
                    nc.gpsimd.tensor_tensor(d, d, s2, ALU.add).then_inc(merged, 1)
                    v = after("squared", ph, i, j)
                    pool.wait_ge(sq_added, v + 1)
                    add_square(g, squared, v, sq_added)
                elif k == "accum":
                    pool.wait_ge(summed, n + 1 + 2)
                    d = tiles(PJ, t0 + (16 if ph.name.startswith("ffn") else 0), 2)
                    pool.wait_ge(epi_done, n + 2)
                    apart()
                    nc.gpsimd.tensor_tensor(d, d, s2, ALU.add).then_inc(epi_done, 1)
                elif k == "accsq":
                    pool.wait_ge(summed, n + 1 + 2)
                    d = tiles(PJ, t0 + 16, 2)
                    apart()
                    nc.gpsimd.tensor_tensor(d, d, s2, ALU.add).then_inc(merged, 1)
                    pool.wait_ge(merged, after("merged", ph, i, j))
                    pool.wait_ge(epi_done, n + 2)
                    pool.sem_inc(epi_done, 1)
                    v = after("squared", ph, i, j)
                    pool.wait_ge(sq_added, v + 1)
                    add_square(g, squared, v, sq_added)
                elif k == "mix":
                    v = after("squared", ph, i, j)
                    pool.wait_ge(sq_added, v + 1)
                    add_square(g, squared, v, sq_added)
                elif k == "final":
                    pool.wait_ge(scaled, after("scaled", ph, i, j))
                    d = tiles(PJ, t0, 2)
                    pool.wait_ge(epi_done, n + 2)
                    apart()
                    nc.gpsimd.tensor_tensor(d, d, s2, ALU.add).then_inc(epi_done, 1)

            def run(name):
                ph = BY[name]

                def body(i):
                    for j in range(ph.U):
                        epilogue(ph, i, j)
                over(pool, body, 0, ph.bodies)

            def reset(n):
                if n:
                    pool.wait_ge(ssq_ready, n)
                nc.gpsimd.memset(sqacc[:], 0.0).then_inc(acc_reset, 1)
                pool.wait_ge(acc_reset, n + 1)

            pool.sem_inc(sq_added, 2)
            reset(0)
            for b in range(8):
                if b:
                    pool.wait_ge(sq0_added, b)
                add_square(b % 2, sq0_ready, b + 1, sq0_added)
            nc.gpsimd.memset(cbuf[:, 0:1024], 0.0).then_inc(bd_zeroed, 1)
            pool.wait_ge(bd_zeroed, 1)
            pool.dma_start(w_f, rows(A["w_in"])[:, :, N_F:N_F + HEADS]).then_inc(in_wf, 16)
            pool.dma_start(cbuf[:, 1664:2192], A["first"]).then_inc(in_c1, 16)
            for c in range(BT):
                pool.dma_start(pool_w[:, c, :], A["pool_w"][c]).then_inc(in_c1, 16)
                for e in range(2):
                    hs = slice(HD * e, HD * e + HD)
                    pool.dma_start(wr_bd[hs, c, hs], A["lru_wr"][2 * c + e]).then_inc(in_c1, 16)
                    pool.dma_start(wi_bd[hs, c, hs], A["lru_wi"][2 * c + e]).then_inc(in_c1, 16)
            pool.wait_ge(epi_done, BY["proj_b"].unit0 + 2)
            for c in range(BT):
                if c:
                    pool.wait_ge(pooled, c)
                src = PJ[:, 4 + c, :]
                for m in range(c + 1):
                    sh = 1 << m
                    dst = tile(G, 23 + m % 2)
                    nc.gpsimd.tensor_copy(dst[:, 0:sh], src[:, 0:sh])
                    link(nc.gpsimd.tensor_tensor(dst[:, sh:S], src[:, sh:S], src[:, 0:S - sh], ALU.add))
                    src = dst
                pool.sem_inc(win_ready, 1)
            pool.wait_ge(lru_ps, BT)
            pool.dma_start(cbuf[0:HEADS, 0:1024], A["sel"]).then_inc(in_sel, 16)
            pool.wait_ge(y_done, 16)
            pool.dma_start(cbuf[:, 0:1408], A["second"]).then_inc(in_c2, 16)
            for q in range(4):
                run(f"mix_a{q}")
                if q == 1:
                    pool.wait_ge(epi_done, BY["mix_a1"].unit0 + 8 + 2)
                    pool.dma_start(resid, x_v).then_inc(in_resid, 16)
            reset(1)
            pool.wait_ge(in_resid, 16)
            run("w_out")
            reset(2)
            for g in range(4):
                run(f"mlp_down{g}")
            pool.wait_ge(y_done, 24)
            pool.dma_start(PJ[:, 32:34, :], p_v).then_inc(in_p, 16)
            for half in range(2):
                run(f"mix_b{half}")
            reset(3)
            run("w_out2")

            def post_norm(n, first, squares):
                if squares:
                    reset(n + 1)
                for b in range(9):
                    if b < 8:
                        pool.wait_ge(pn_t, first // 2 + b + 1)
                        d = PJ[:, 2 * b:2 * b + 2, :]
                        nc.gpsimd.tensor_tensor(d, d, summ[:, b % 2], ALU.add).then_inc(pn_r, 1)
                    if b and squares:
                        if b > 1:
                            pool.wait_ge(pn_added, b - 1)
                        add_square((b - 1) % 2, pn_sq, b, pn_added)
            post_norm(3, 0, True)
            reset(5)
            run("ffn_down1")
            run("ffn_down2")
            post_norm(5, 16, False)
            run("ple_gate")


def kernel(**inputs):
    import concourse.bacc as _bacc
    from concourse.bass_utils import run_bass_kernel_spmd as _run

    a = {k: np.asarray(v) for k, v in inputs.items()}
    cols, npar = param_columns()

    def columns(v):
        v = v.reshape(-1, v.shape[-1] // P, P)
        return v.transpose(2, 0, 1).reshape(P, -1)

    fb = np.zeros((P, 1), np.float32)
    fb[0:HEADS, 0] = a["forget_b"][0]
    params = np.concatenate(
        [columns(a[k]) for k in ("norm_mix_g", "norm_mlp_g", "g_mix_pre_2", "g_mix_post_2", "g_ffn_pre_2",
                                 "g_ffn_post_2")]
        + [columns(a["lru_conv_w"][0]), columns(a["lru_conv_b"]), columns(a["lru_br"]), columns(a["lru_bi"]),
           columns(a["lru_lambda"]), columns(a["pool_scale"]), columns(a["sconv_w"][0]),
           np.concatenate([a["q_norm_g"], a["q_norm_g"]], 1).T, np.concatenate([a["k_norm_g"], a["k_norm_g"]], 1).T,
           fb, columns(a["conv_w_2"][0]), columns(a["conv_b_2"])], 1)
    common, first, sel, second = constants()
    arrays = {
        "x_t": a["x"][0].T, "p_t": a["p_2"][0, 0].T, "params": params, "common": common, "first": first,
        "sel": sel, "second": second, "w_in": a["w_in"][0], "w_branch": a["w_branch"][0].reshape(D, D),
        "lru_wr": a["lru_wr"][0], "lru_wi": a["lru_wi"][0], "pool_w": a["pool_w"][0],
    }
    for k in ("w_out", "w_mlp_up", "w_mlp_down", "w_in_2", "w_branch_a_2", "w_branch_b_2", "w_out_2", "w_up_2",
              "w_down_2", "w_ple_in_2", "w_ple_gate_2"):
        arrays[k] = a[k][0]
    arrays = {k: np.ascontiguousarray(v) for k, v in arrays.items()}

    nc = _bacc.Bacc("TRN2", target_bir_lowering=False, num_devices=1)
    A = {k: nc.dram_tensor("in_" + k, v.shape, F32, kind="ExternalInput").ap() for k, v in arrays.items()}
    out = nc.dram_tensor("out_t", (D, S), F32, kind="ExternalOutput").ap()
    build(nc, A, out)
    r = _run(nc, [{"in_" + k: v for k, v in arrays.items()}], core_ids=[0])
    return np.ascontiguousarray(np.asarray(r.results[0]["out_t"]).T)[None]
```
